# Optimizing a Trainium2 kernel written in Bass

```python
import math
import jax
import jax.numpy as jnp
from jax import lax
import numpy as np

D_MODEL = 1024
BATCH = 1
SEQ = 256
DEPTH = 2

HEAD_DIM = 64
GDN_WIDTH = 3 * D_MODEL // 8
CONV_WIDTH = D_MODEL // 4
FOX_WIDTH = D_MODEL - GDN_WIDTH - CONV_WIDTH
MIX_WIDTH = GDN_WIDTH + CONV_WIDTH + FOX_WIDTH
GDN_HEADS = GDN_WIDTH // HEAD_DIM
FOX_HEADS = FOX_WIDTH // HEAD_DIM
GDN_SHORT_CONV = 4
GDN_CHUNK = 64
CONV_KERNEL = 31
FOX_BLOCK = 128
FFN_DENSE = ((8 * D_MODEL // 3 + 127) // 128) * 128
N_EXPERTS = 8
TOP_K = 2
FFN_EXPERT = 7 * D_MODEL // 2
MOE_BLOCK = 128
N_DENSE = (DEPTH + 1) // 2
N_MOE = DEPTH // 2
DEEPNORM_ALPHA = (2 * DEPTH) ** 0.25
DEEPNORM_BETA = (8 * DEPTH) ** -0.25
LN_EPS = 1e-5
NORM_EPS = 1e-6
IN_SIZES = (GDN_WIDTH, GDN_WIDTH, GDN_WIDTH, GDN_HEADS, GDN_HEADS, GDN_WIDTH,
            2 * CONV_WIDTH,
            FOX_WIDTH, FOX_WIDTH, FOX_WIDTH, FOX_HEADS)
IN_COLS = sum(IN_SIZES)


def layer_norm(x, g, b):
    xf = x.astype(jnp.float32)
    mu = xf.mean(-1, keepdims=True)
    var = jnp.square(xf - mu).mean(-1, keepdims=True)
    return ((xf - mu) * lax.rsqrt(var + LN_EPS) * g.astype(jnp.float32) + b.astype(jnp.float32)).astype(x.dtype)

def rms_norm_f32(x, g):
    xf = x.astype(jnp.float32)
    return xf * lax.rsqrt(jnp.square(xf).mean(-1, keepdims=True) + NORM_EPS) * g.astype(jnp.float32)

def l2_normalize(x):
    return x * lax.rsqrt(jnp.sum(jnp.square(x), -1, keepdims=True) + NORM_EPS)

def split_columns(p, sizes):
    cuts = np.cumsum(np.array(sizes))[:-1].tolist()
    return jnp.split(p, cuts, axis=-1)

def causal_depthwise_conv(x, w):
    k_width, channels = w.shape
    return lax.conv_general_dilated(
        x, w[:, None, :], window_strides=(1,), padding=[(k_width - 1, 0)],
        dimension_numbers=('NWC', 'WIO', 'NWC'), feature_group_count=channels)

def gated_delta_rule(q, k, v, g, beta):
    B, T, H, dk = q.shape
    dv = v.shape[-1]
    C = GDN_CHUNK
    n = T // C
    f32 = jnp.float32
    q = l2_normalize(q.astype(f32)) * dk ** -0.5
    k = l2_normalize(k.astype(f32))
    v = v.astype(f32)

    def chunks(t):
        return t.reshape(B, n, C, H, -1).transpose(1, 0, 3, 2, 4)

    qc, kc, vc = chunks(q), chunks(k), chunks(v)
    gc = jnp.cumsum(chunks(g.astype(f32)[..., None])[..., 0], axis=-1)
    bc = chunks(beta.astype(f32)[..., None])
    causal = jnp.tril(jnp.ones((C, C), bool))
    strict = jnp.tril(jnp.ones((C, C), bool), -1)
    diff = gc[..., :, None] - gc[..., None, :]
    decay = jnp.where(causal, jnp.exp(jnp.where(causal, diff, 0.0)), 0.0)
    kb = kc * bc
    lower = jnp.where(strict, jnp.einsum('nbhcd,nbhsd->nbhcs', kb, kc) * decay, 0.0)
    eye = jnp.eye(C, dtype=f32)
    t_inv = lax.linalg.triangular_solve(lower + eye, jnp.broadcast_to(eye, lower.shape),
                                        left_side=True, lower=True, unit_diagonal=True)
    u = jnp.einsum('nbhcs,nbhsd->nbhcd', t_inv, vc * bc)
    w = jnp.einsum('nbhcs,nbhsd->nbhcd', t_inv, kb * jnp.exp(gc)[..., None])
    a_intra = jnp.where(causal, jnp.einsum('nbhcd,nbhsd->nbhcs', qc, kc) * decay, 0.0)

    def step(state, inp):
        q_i, k_i, u_i, w_i, a_i, g_i = inp
        v_new = u_i - jnp.einsum('bhck,bhkv->bhcv', w_i, state)
        o_i = (jnp.einsum('bhck,bhkv->bhcv', q_i * jnp.exp(g_i)[..., None], state)
               + jnp.einsum('bhcs,bhsv->bhcv', a_i, v_new))
        g_last = g_i[..., -1]
        state = (state * jnp.exp(g_last)[..., None, None]
                 + jnp.einsum('bhck,bhcv->bhkv', k_i * jnp.exp(g_last[..., None] - g_i)[..., None], v_new))
        return state, o_i

    s0 = jnp.zeros((B, H, dk, dv), f32)
    _, o = lax.scan(step, s0, (qc, kc, u, w, a_intra, gc))
    return o.transpose(1, 0, 3, 2, 4).reshape(B, T, H, dv)

def forgetting_attention(q, k, v, log_f):
    B, T, H, d = q.shape
    f32 = jnp.float32
    nb = T // FOX_BLOCK
    c = jnp.cumsum(log_f.astype(f32), axis=1)
    qb = (q.astype(f32) * d ** -0.5).reshape(B, nb, FOX_BLOCK, H, d).transpose(1, 0, 3, 2, 4)
    cq = c.reshape(B, nb, FOX_BLOCK, H).transpose(1, 0, 3, 2)
    kt = k.astype(f32).transpose(0, 2, 1, 3)
    vt = v.astype(f32).transpose(0, 2, 1, 3)
    ck = c.transpose(0, 2, 1)
    key_pos = jnp.arange(T)

    def block(args):
        q_blk, cq_blk, i = args
        q_pos = i * FOX_BLOCK + jnp.arange(FOX_BLOCK)
        s = jnp.einsum('bhqd,bhkd->bhqk', q_blk, kt) + cq_blk[..., None] - ck[:, :, None, :]
        s = jnp.where(key_pos[None, :] <= q_pos[:, None], s, -jnp.inf)
        p = jax.nn.softmax(s, axis=-1)
        return jnp.einsum('bhqk,bhkd->bhqd', p, vt)

    o = lax.map(block, (qb, cq, jnp.arange(nb)))
    return o.transpose(1, 0, 3, 2, 4).reshape(B, T, H, d)

def hybrid_mixer(x, w_in, mix_scale, w_out, gdn_conv_w, gdn_a_log, gdn_dt_bias, gdn_norm_w,
                 cnv_dw_w, cnv_dw_b, cnv_ln_g, cnv_ln_b, fox_f_bias):
    B, T, _ = x.shape
    dt = x.dtype
    f32 = jnp.float32
    proj = jnp.einsum('btd,de->bte', x, w_in)
    (a_q, a_k, a_v, a_decay, a_beta, a_gate, c_glu, f_q, f_k, f_v, f_forget) = split_columns(proj, IN_SIZES)

    def heads(t, h):
        return t.reshape(B, T, h, HEAD_DIM)

    qkv = jax.nn.silu(causal_depthwise_conv(jnp.concatenate([a_q, a_k, a_v], -1), gdn_conv_w))
    a_q, a_k, a_v = jnp.split(qkv, 3, axis=-1)
    log_decay = -jnp.exp(gdn_a_log.astype(f32)) * jax.nn.softplus(a_decay.astype(f32) + gdn_dt_bias.astype(f32))
    beta = jax.nn.sigmoid(a_beta.astype(f32))
    o_a = gated_delta_rule(heads(a_q, GDN_HEADS), heads(a_k, GDN_HEADS), heads(a_v, GDN_HEADS), log_decay, beta)
    o_a = (rms_norm_f32(o_a, gdn_norm_w) * jax.nn.silu(heads(a_gate, GDN_HEADS).astype(f32))).reshape(B, T, GDN_WIDTH).astype(dt)

    glu_a, glu_b = jnp.split(c_glu, 2, axis=-1)
    u = glu_a * jax.nn.sigmoid(glu_b)
    u = causal_depthwise_conv(u, cnv_dw_w) + cnv_dw_b
    o_b = jax.nn.silu(layer_norm(u, cnv_ln_g, cnv_ln_b))

    log_f = jax.nn.log_sigmoid(f_forget.astype(f32) + fox_f_bias.astype(f32))
    o_c = forgetting_attention(heads(f_q, FOX_HEADS), heads(f_k, FOX_HEADS), heads(f_v, FOX_HEADS), log_f)
    o_c = o_c.reshape(B, T, FOX_WIDTH).astype(dt)

    mixed = jnp.concatenate([o_a, o_b, o_c], axis=-1) * mix_scale
    return jnp.einsum('bte,ed->btd', mixed, w_out)

def swiglu(x, w1, w3, w2):
    h = jax.nn.silu(jnp.einsum('btd,df->btf', x, w1)) * jnp.einsum('btd,df->btf', x, w3)
    return jnp.einsum('btf,fd->btd', h, w2)

def moe_swiglu(x, w_router, w1, w3, w2):
    B, T, D = x.shape
    xf = x.reshape(-1, D)
    n_tok = xf.shape[0]
    n_asg = n_tok * TOP_K
    logits = jnp.einsum('nd,de->ne', xf, w_router).astype(jnp.float32)
    top_logits, top_idx = lax.top_k(logits, TOP_K)
    gates = jax.nn.softmax(top_logits, axis=-1)
    e_flat = top_idx.reshape(-1)
    order = jnp.argsort(e_flat)
    e_sorted = e_flat[order]
    sizes = jnp.bincount(e_flat, length=N_EXPERTS).astype(jnp.int32)
    padded = ((sizes + MOE_BLOCK - 1) // MOE_BLOCK) * MOE_BLOCK
    pad_end = jnp.cumsum(padded)
    pad_start = pad_end - padded
    start = jnp.cumsum(sizes) - sizes
    rank = jnp.arange(n_asg, dtype=jnp.int32) - start[e_sorted]
    dest = pad_start[e_sorted] + rank
    n_blocks = (n_asg + MOE_BLOCK - 1) // MOE_BLOCK + N_EXPERTS
    rows = n_blocks * MOE_BLOCK
    tok_pad = jnp.full((rows,), n_tok, jnp.int32).at[dest].set((order // TOP_K).astype(jnp.int32))
    gate_pad = jnp.zeros((rows,), jnp.float32).at[dest].set(gates.reshape(-1)[order])
    block_start = jnp.arange(n_blocks, dtype=jnp.int32) * MOE_BLOCK
    block_expert = jnp.minimum(jnp.searchsorted(pad_end, block_start, side='right'), N_EXPERTS - 1)
    x_ext = jnp.concatenate([xf, jnp.zeros((1, D), xf.dtype)], axis=0)
    x_blocks = x_ext[tok_pad].reshape(n_blocks, MOE_BLOCK, D)

    def expert_block(args):
        xb, e = args
        h = jax.nn.silu(xb @ w1[e]) * (xb @ w3[e])
        return h @ w2[e]

    y = lax.map(expert_block, (x_blocks, block_expert)).reshape(rows, D)
    y = y * gate_pad[:, None].astype(y.dtype)
    out = jnp.zeros((n_tok + 1, D), y.dtype).at[tok_pad].add(y)[:n_tok]
    return out.reshape(B, T, D)

def first_inputs(seed: int = 0) -> dict:
    key = jax.random.key(seed)
    ks = jax.random.split(key, 26)
    f32 = jnp.float32
    nrm = jax.random.normal
    x = nrm(ks[0], (BATCH, SEQ, D_MODEL), f32)
    w_in = nrm(ks[1], (DEPTH, D_MODEL, IN_COLS), f32) * D_MODEL ** -0.5
    mix_scale = 1.0 + 0.05 * nrm(ks[2], (DEPTH, MIX_WIDTH), f32)
    w_out = nrm(ks[3], (DEPTH, MIX_WIDTH, D_MODEL), f32) * (MIX_WIDTH ** -0.5 * DEEPNORM_BETA)
    gdn_conv_w = nrm(ks[4], (DEPTH, GDN_SHORT_CONV, 3 * GDN_WIDTH), f32) * GDN_SHORT_CONV ** -0.5
    gdn_a_log = jnp.log(jax.random.uniform(ks[5], (DEPTH, GDN_HEADS), f32, 1.0, 16.0))
    dt_init = jnp.exp(jax.random.uniform(ks[6], (DEPTH, GDN_HEADS), f32, math.log(1e-3), math.log(1e-1)))
    gdn_dt_bias = dt_init + jnp.log(-jnp.expm1(-dt_init))
    gdn_norm_w = 1.0 + 0.05 * nrm(ks[7], (DEPTH, HEAD_DIM), f32)
    cnv_dw_w = nrm(ks[8], (DEPTH, CONV_KERNEL, CONV_WIDTH), f32) * CONV_KERNEL ** -0.5
    cnv_dw_b = 0.02 * nrm(ks[9], (DEPTH, CONV_WIDTH), f32)
    cnv_ln_g = 1.0 + 0.05 * nrm(ks[10], (DEPTH, CONV_WIDTH), f32)
    cnv_ln_b = 0.02 * nrm(ks[11], (DEPTH, CONV_WIDTH), f32)
    fox_f_bias = 3.0 + 0.5 * nrm(ks[12], (DEPTH, FOX_HEADS), f32)
    ln_mix_g = 1.0 + 0.05 * nrm(ks[13], (DEPTH, D_MODEL), f32)
    ln_mix_b = 0.02 * nrm(ks[14], (DEPTH, D_MODEL), f32)
    ln_ffn_g = 1.0 + 0.05 * nrm(ks[15], (DEPTH, D_MODEL), f32)
    ln_ffn_b = 0.02 * nrm(ks[16], (DEPTH, D_MODEL), f32)
    ffn_w1 = nrm(ks[17], (N_DENSE, D_MODEL, FFN_DENSE), f32) * D_MODEL ** -0.5
    ffn_w3 = nrm(ks[18], (N_DENSE, D_MODEL, FFN_DENSE), f32) * D_MODEL ** -0.5
    ffn_w2 = nrm(ks[19], (N_DENSE, FFN_DENSE, D_MODEL), f32) * (FFN_DENSE ** -0.5 * DEEPNORM_BETA)
    moe_router = nrm(ks[20], (N_MOE, D_MODEL, N_EXPERTS), f32) * D_MODEL ** -0.5
    moe_w1 = nrm(ks[21], (N_MOE, N_EXPERTS, D_MODEL, FFN_EXPERT), f32) * D_MODEL ** -0.5
    moe_w3 = nrm(ks[22], (N_MOE, N_EXPERTS, D_MODEL, FFN_EXPERT), f32) * D_MODEL ** -0.5
    moe_w2 = nrm(ks[23], (N_MOE, N_EXPERTS, FFN_EXPERT, D_MODEL), f32) * (FFN_EXPERT ** -0.5 * DEEPNORM_BETA)
    return {'x': x, 'w_in': w_in, 'mix_scale': mix_scale, 'w_out': w_out,
            'gdn_conv_w': gdn_conv_w, 'gdn_a_log': gdn_a_log, 'gdn_dt_bias': gdn_dt_bias, 'gdn_norm_w': gdn_norm_w,
            'cnv_dw_w': cnv_dw_w, 'cnv_dw_b': cnv_dw_b, 'cnv_ln_g': cnv_ln_g, 'cnv_ln_b': cnv_ln_b,
            'fox_f_bias': fox_f_bias,
            'ln_mix_g': ln_mix_g, 'ln_mix_b': ln_mix_b, 'ln_ffn_g': ln_ffn_g, 'ln_ffn_b': ln_ffn_b,
            'ffn_w1': ffn_w1, 'ffn_w3': ffn_w3, 'ffn_w2': ffn_w2,
            'moe_router': moe_router, 'moe_w1': moe_w1, 'moe_w3': moe_w3, 'moe_w2': moe_w2}

def first_block(x, w_in, mix_scale, w_out, gdn_conv_w, gdn_a_log, gdn_dt_bias, gdn_norm_w,
              cnv_dw_w, cnv_dw_b, cnv_ln_g, cnv_ln_b, fox_f_bias,
              ln_mix_g, ln_mix_b, ln_ffn_g, ln_ffn_b,
              ffn_w1, ffn_w3, ffn_w2, moe_router, moe_w1, moe_w3, moe_w2):
    for l in range(DEPTH):
        mix = hybrid_mixer(x, w_in[l], mix_scale[l], w_out[l], gdn_conv_w[l], gdn_a_log[l], gdn_dt_bias[l],
                           gdn_norm_w[l], cnv_dw_w[l], cnv_dw_b[l], cnv_ln_g[l], cnv_ln_b[l], fox_f_bias[l])
        x = layer_norm(DEEPNORM_ALPHA * x + mix, ln_mix_g[l], ln_mix_b[l])
        if l % 2 == 0:
            ff = swiglu(x, ffn_w1[l // 2], ffn_w3[l // 2], ffn_w2[l // 2])
        else:
            ff = moe_swiglu(x, moe_router[l // 2], moe_w1[l // 2], moe_w3[l // 2], moe_w2[l // 2])
        x = layer_norm(DEEPNORM_ALPHA * x + ff, ln_ffn_g[l], ln_ffn_b[l])
    return x


GRID_W = 64
CTX_LEN = 256
N_MIXERS = 4
Q_BLOCK = 128
ROPE_BASE = 10000.0
EPS = 1e-6
NEG_INF = -1e30

GQA_HEADS = 16
GQA_KV_HEADS = 4
GQA_HEAD_DIM = 64
MLA_HEADS = 16
MLA_NOPE_DIM = 64
MLA_ROPE_DIM = 32
MLA_V_DIM = 64
MLA_Q_LORA = 384
MLA_KV_LORA = 256
DIFF_HEADS = 8
DIFF_HEAD_DIM = 64
NA_HEADS = 16
NA_HEAD_DIM = 64
NA_ROWS = 8
NA_COLS = 16
NA_QROWS = Q_BLOCK // GRID_W
FFN_DIM = 2816


def rms_norm(x, g):
    xf = x.astype(jnp.float32)
    y = xf * lax.rsqrt(jnp.mean(xf * xf, axis=-1, keepdims=True) + EPS)
    return (y * g.astype(jnp.float32)).astype(x.dtype)

def norm_modulate(h, g, shift, scale):
    return rms_norm(h, g) * (1 + scale) + shift

def softmax_f32(s):
    return jax.nn.softmax(s.astype(jnp.float32), axis=-1)

def axial_rope(n_tokens, rot_dim, dtype):
    t = jnp.arange(n_tokens)
    row = (t // GRID_W).astype(jnp.float32)
    col = (t % GRID_W).astype(jnp.float32)
    half = rot_dim // 2
    inv = ROPE_BASE ** (-jnp.arange(0, half, 2, dtype=jnp.float32) / half)
    ar, ac = row[:, None] * inv, col[:, None] * inv
    ang = jnp.concatenate([ar, ar, ac, ac], axis=-1)
    return jnp.cos(ang).astype(dtype), jnp.sin(ang).astype(dtype)

def apply_rope(x, cos, sin):
    x1, x2, x3, x4 = jnp.split(x, 4, axis=-1)
    rot = jnp.concatenate([-x2, x1, -x4, x3], axis=-1)
    shape = (cos.shape[0],) + (1,) * (x.ndim - 3) + (cos.shape[1],)
    return x * cos.reshape(shape) + rot * sin.reshape(shape)

def sweep_query_blocks(fn, *qs):
    b, t = qs[0].shape[:2]
    nb = t // Q_BLOCK
    blocks = tuple(jnp.moveaxis(q.reshape(b, nb, Q_BLOCK, *q.shape[2:]), 1, 0) for q in qs)
    out = lax.map(lambda qb: fn(*qb), blocks)
    return jnp.moveaxis(out, 0, 1).reshape(b, t, *out.shape[3:])

def gqa_mixer(hx, hc, w_in, q_g, k_g, w_out, ctx_out):
    b, t, d = hx.shape
    grp = GQA_HEADS // GQA_KV_HEADS
    splits = [GQA_HEADS * GQA_HEAD_DIM, (GQA_HEADS + GQA_KV_HEADS) * GQA_HEAD_DIM]

    def project(h):
        n = h.shape[1]
        q, k, v = jnp.split(h @ w_in, splits, axis=-1)
        q = rms_norm(q.reshape(b, n, GQA_KV_HEADS, grp, GQA_HEAD_DIM), q_g)
        k = rms_norm(k.reshape(b, n, GQA_KV_HEADS, GQA_HEAD_DIM), k_g)
        return q, k, v.reshape(b, n, GQA_KV_HEADS, GQA_HEAD_DIM)

    qx, kx, vx = project(hx)
    qc, kc, vc = project(hc)
    cos, sin = axial_rope(t, GQA_HEAD_DIM, hx.dtype)
    qx, kx = apply_rope(qx, cos, sin), apply_rope(kx, cos, sin)
    k_all = jnp.concatenate([kc, kx], axis=1)
    v_all = jnp.concatenate([vc, vx], axis=1)
    scale = GQA_HEAD_DIM ** -0.5

    def attend(q, k, v):
        s = jnp.einsum('bqhgd,bkhd->bhgqk', q, k) * scale
        p = softmax_f32(s).astype(v.dtype)
        return jnp.einsum('bhgqk,bkhd->bqhgd', p, v)

    out_x = sweep_query_blocks(lambda qb: attend(qb, k_all, v_all), qx).reshape(b, t, d) @ w_out
    out_c = attend(qc, kc, vc).reshape(b, hc.shape[1], d) @ w_out if ctx_out else None
    return out_x, out_c

def mla_mixer(hx, hc, w_in, q_norm_g, kv_norm_g, w_uq, w_ukv, w_out, ctx_out):
    b, t, d = hx.shape
    qk_dim = MLA_NOPE_DIM + MLA_ROPE_DIM

    def project(h):
        n = h.shape[1]
        cq, ckv, k_rope = jnp.split(h @ w_in, [MLA_Q_LORA, MLA_Q_LORA + MLA_KV_LORA], axis=-1)
        q = (rms_norm(cq, q_norm_g) @ w_uq).reshape(b, n, MLA_HEADS, qk_dim)
        kv = (rms_norm(ckv, kv_norm_g) @ w_ukv).reshape(b, n, MLA_HEADS, MLA_NOPE_DIM + MLA_V_DIM)
        q_nope, q_rope = jnp.split(q, [MLA_NOPE_DIM], axis=-1)
        k_nope, v = jnp.split(kv, [MLA_NOPE_DIM], axis=-1)
        return q_nope, q_rope, k_nope, k_rope, v

    qnx, qrx, knx, krx, vx = project(hx)
    qnc, qrc, knc, krc, vc = project(hc)
    cos, sin = axial_rope(t, MLA_ROPE_DIM, hx.dtype)
    qrx, krx = apply_rope(qrx, cos, sin), apply_rope(krx, cos, sin)
    kn_all = jnp.concatenate([knc, knx], axis=1)
    kr_all = jnp.concatenate([krc, krx], axis=1)
    v_all = jnp.concatenate([vc, vx], axis=1)
    scale = qk_dim ** -0.5

    def attend(qn, qr, kn, kr, v):
        s = (jnp.einsum('bqhd,bkhd->bhqk', qn, kn) + jnp.einsum('bqhd,bkd->bhqk', qr, kr)) * scale
        p = softmax_f32(s).astype(v.dtype)
        return jnp.einsum('bhqk,bkhd->bqhd', p, v)

    ox = sweep_query_blocks(lambda qn, qr: attend(qn, qr, kn_all, kr_all, v_all), qnx, qrx)
    out_x = ox.reshape(b, t, MLA_HEADS * MLA_V_DIM) @ w_out
    out_c = attend(qnc, qrc, knc, krc, vc).reshape(b, hc.shape[1], MLA_HEADS * MLA_V_DIM) @ w_out if ctx_out else None
    return out_x, out_c

def diff_mixer(hx, hc, w_in, lam, subln_g, w_out, layer_idx, ctx_out):
    b, t, d = hx.shape
    lambda_init = 0.8 - 0.6 * math.exp(-0.3 * layer_idx)
    lf = lam.astype(jnp.float32)
    lam_full = jnp.exp(jnp.sum(lf[0] * lf[1])) - jnp.exp(jnp.sum(lf[2] * lf[3])) + lambda_init

    def project(h):
        n = h.shape[1]
        q, k, v = jnp.split(h @ w_in, 3, axis=-1)
        q = q.reshape(b, n, DIFF_HEADS, 2, DIFF_HEAD_DIM)
        k = k.reshape(b, n, DIFF_HEADS, 2, DIFF_HEAD_DIM)
        return q, k, v.reshape(b, n, DIFF_HEADS, 2 * DIFF_HEAD_DIM)

    qx, kx, vx = project(hx)
    qc, kc, vc = project(hc)
    cos, sin = axial_rope(t, DIFF_HEAD_DIM, hx.dtype)
    qx, kx = apply_rope(qx, cos, sin), apply_rope(kx, cos, sin)
    k_all = jnp.concatenate([kc, kx], axis=1)
    v_all = jnp.concatenate([vc, vx], axis=1)
    scale = DIFF_HEAD_DIM ** -0.5

    def attend(q, k, v):
        s = jnp.einsum('bqhjd,bkhjd->bhjqk', q, k) * scale
        p = softmax_f32(s)
        p = p[:, :, 0] - lam_full * p[:, :, 1]
        o = jnp.einsum('bhqk,bkhe->bqhe', p.astype(v.dtype), v)
        return rms_norm(o, subln_g) * (1 - lambda_init)

    out_x = sweep_query_blocks(lambda qb: attend(qb, k_all, v_all), qx).reshape(b, t, d) @ w_out
    out_c = attend(qc, kc, vc).reshape(b, hc.shape[1], d) @ w_out if ctx_out else None
    return out_x, out_c

def na_mixer(hx, hc, w_in, rpb, w_out, ctx_out):
    b, t, d = hx.shape
    rows = t // GRID_W
    win_rows = min(NA_ROWS, rows)
    band_rows = min(win_rows + 1, rows)
    band = band_rows * GRID_W
    n_ctx = hc.shape[1]

    def project(h):
        n = h.shape[1]
        q, k, v = jnp.split(h @ w_in, 3, axis=-1)
        return tuple(a.reshape(b, n, NA_HEADS, NA_HEAD_DIM) for a in (q, k, v))

    qx, kx, vx = project(hx)
    qc, kc, vc = project(hc)
    scale = NA_HEAD_DIM ** -0.5
    k_grid = kx.reshape(b, rows, GRID_W, NA_HEADS, NA_HEAD_DIM)
    v_grid = vx.reshape(b, rows, GRID_W, NA_HEADS, NA_HEAD_DIM)
    nb = t // Q_BLOCK
    q_blocks = jnp.moveaxis(qx.reshape(b, nb, Q_BLOCK, NA_HEADS, NA_HEAD_DIM), 1, 0)
    q_off, k_off = jnp.arange(Q_BLOCK), jnp.arange(band)
    q_dr, q_col = q_off // GRID_W, q_off % GRID_W
    k_dr, k_col = k_off // GRID_W, k_off % GRID_W
    col_start = jnp.clip(q_col - NA_COLS // 2, 0, GRID_W - NA_COLS)
    col_in = (k_col[None, :] >= col_start[:, None]) & (k_col[None, :] < col_start[:, None] + NA_COLS)
    dc_idx = jnp.clip(k_col[None, :] - q_col[:, None] + NA_COLS - 1, 0, 2 * NA_COLS - 2)

    def block(args):
        j, qb = args
        r = j * NA_QROWS + q_dr
        row_start = jnp.clip(r - win_rows // 2, 0, rows - win_rows)
        b0 = jnp.minimum(row_start[0], rows - band_rows)
        k_band = lax.dynamic_slice_in_dim(k_grid, b0, band_rows, axis=1).reshape(b, band, NA_HEADS, NA_HEAD_DIM)
        v_band = lax.dynamic_slice_in_dim(v_grid, b0, band_rows, axis=1).reshape(b, band, NA_HEADS, NA_HEAD_DIM)
        k_row = b0 + k_dr
        in_win = col_in & (k_row[None, :] >= row_start[:, None]) & (k_row[None, :] < row_start[:, None] + win_rows)
        dr_idx = jnp.clip(k_row[None, :] - r[:, None] + NA_ROWS - 1, 0, 2 * NA_ROWS - 2)
        bias = rpb[:, dr_idx, dc_idx].astype(jnp.float32)
        s_lat = jnp.einsum('bqhd,bkhd->bhqk', qb, k_band).astype(jnp.float32) * scale + bias
        s_lat = jnp.where(in_win, s_lat, NEG_INF)
        s_ctx = jnp.einsum('bqhd,bkhd->bhqk', qb, kc).astype(jnp.float32) * scale
        p = softmax_f32(jnp.concatenate([s_ctx, s_lat], axis=-1)).astype(vx.dtype)
        return (jnp.einsum('bhqk,bkhd->bqhd', p[..., :n_ctx], vc)
                + jnp.einsum('bhqk,bkhd->bqhd', p[..., n_ctx:], v_band))

    ox = lax.map(block, (jnp.arange(nb), q_blocks))
    out_x = jnp.moveaxis(ox, 0, 1).reshape(b, t, d) @ w_out
    if ctx_out:
        s = jnp.einsum('bqhd,bkhd->bhqk', qc, kc) * scale
        p = softmax_f32(s).astype(vc.dtype)
        out_c = jnp.einsum('bhqk,bkhd->bqhd', p, vc).reshape(b, n_ctx, d) @ w_out
    else:
        out_c = None
    return out_x, out_c

def dwconv_centred(u, w, bias):
    p = jnp.pad(u, ((0, 0), (1, 1), (0, 0)))
    return p[:, :-2] * w[0] + p[:, 1:-1] * w[1] + p[:, 2:] * w[2] + bias

def conv_ffn(h, w_up, conv_w, conv_b, w_down):
    u = dwconv_centred(h @ w_up, conv_w, conv_b)
    val, gate = jnp.split(u, 2, axis=-1)
    return (jax.nn.silu(gate) * val) @ w_down

def second_inputs(seed: int = 0) -> dict:
    key = jax.random.key(seed)
    ks = iter(jax.random.split(key, 32))
    D = D_MODEL

    def nrm(shape, scale=1.0):
        return jax.random.normal(next(ks), shape, jnp.float32) * scale

    def gain(shape):
        return 1.0 + nrm(shape, 0.02)

    la, lb, lc, ld = (len(range(m, DEPTH, N_MIXERS)) for m in range(N_MIXERS))
    gqa_in = (GQA_HEADS + 2 * GQA_KV_HEADS) * GQA_HEAD_DIM
    mla_in = MLA_Q_LORA + MLA_KV_LORA + MLA_ROPE_DIM
    return {
        'x': nrm((BATCH, SEQ, D)),
        'c': nrm((BATCH, D)),
        'ctx': nrm((BATCH, CTX_LEN, D)),
        'c_ctx': nrm((D,)),
        'ada_w': nrm((DEPTH, D, 6 * D), 0.5 * D ** -0.5),
        'ada_b': nrm((DEPTH, 6 * D), 0.02),
        'norm1_g': gain((DEPTH, D)),
        'norm2_g': gain((DEPTH, D)),
        'ffn_w_up': nrm((DEPTH, D, 2 * FFN_DIM), D ** -0.5),
        'ffn_conv_w': nrm((DEPTH, 3, 2 * FFN_DIM), 3 ** -0.5),
        'ffn_conv_b': nrm((DEPTH, 2 * FFN_DIM), 0.02),
        'ffn_w_down': nrm((DEPTH, FFN_DIM, D), FFN_DIM ** -0.5),
        'gqa_w_in': nrm((la, D, gqa_in), D ** -0.5),
        'gqa_q_norm_g': gain((la, GQA_HEAD_DIM)),
        'gqa_k_norm_g': gain((la, GQA_HEAD_DIM)),
        'gqa_w_out': nrm((la, GQA_HEADS * GQA_HEAD_DIM, D), (GQA_HEADS * GQA_HEAD_DIM) ** -0.5),
        'mla_w_in': nrm((lb, D, mla_in), D ** -0.5),
        'mla_q_norm_g': gain((lb, MLA_Q_LORA)),
        'mla_kv_norm_g': gain((lb, MLA_KV_LORA)),
        'mla_w_uq': nrm((lb, MLA_Q_LORA, MLA_HEADS * (MLA_NOPE_DIM + MLA_ROPE_DIM)), MLA_Q_LORA ** -0.5),
        'mla_w_ukv': nrm((lb, MLA_KV_LORA, MLA_HEADS * (MLA_NOPE_DIM + MLA_V_DIM)), MLA_KV_LORA ** -0.5),
        'mla_w_out': nrm((lb, MLA_HEADS * MLA_V_DIM, D), (MLA_HEADS * MLA_V_DIM) ** -0.5),
        'diff_w_in': nrm((lc, D, 3 * D), D ** -0.5),
        'diff_lambda': nrm((lc, 4, DIFF_HEAD_DIM), 0.1),
        'diff_subln_g': gain((lc, 2 * DIFF_HEAD_DIM)),
        'diff_w_out': nrm((lc, D, D), D ** -0.5),
        'na_w_in': nrm((ld, D, 3 * D), D ** -0.5),
        'na_rpb': nrm((ld, NA_HEADS, 2 * NA_ROWS - 1, 2 * NA_COLS - 1), 0.05),
        'na_w_out': nrm((ld, D, D), D ** -0.5),
        'final_norm_g': gain((D,)),
    }

def second_block(x, c, ctx, c_ctx, ada_w, ada_b, norm1_g, norm2_g, ffn_w_up, ffn_conv_w, ffn_conv_b, ffn_w_down,
              gqa_w_in, gqa_q_norm_g, gqa_k_norm_g, gqa_w_out,
              mla_w_in, mla_q_norm_g, mla_kv_norm_g, mla_w_uq, mla_w_ukv, mla_w_out,
              diff_w_in, diff_lambda, diff_subln_g, diff_w_out,
              na_w_in, na_rpb, na_w_out, final_norm_g):
    silu_c = jax.nn.silu(c)
    silu_cc = jax.nn.silu(c_ctx)
    for i in range(DEPTH):
        ctx_out = i < DEPTH - 1
        m, j = i % N_MIXERS, i // N_MIXERS
        sh1, sc1, g1, sh2, sc2, g2 = (a[:, None, :] for a in jnp.split(silu_c @ ada_w[i] + ada_b[i], 6, axis=-1))
        csh1, csc1, cg1, csh2, csc2, cg2 = jnp.split(silu_cc @ ada_w[i] + ada_b[i], 6, axis=-1)
        hx = norm_modulate(x, norm1_g[i], sh1, sc1)
        hc = norm_modulate(ctx, norm1_g[i], csh1, csc1)
        if m == 0:
            ox, oc = gqa_mixer(hx, hc, gqa_w_in[j], gqa_q_norm_g[j], gqa_k_norm_g[j], gqa_w_out[j], ctx_out)
        elif m == 1:
            ox, oc = mla_mixer(hx, hc, mla_w_in[j], mla_q_norm_g[j], mla_kv_norm_g[j], mla_w_uq[j],
                               mla_w_ukv[j], mla_w_out[j], ctx_out)
        elif m == 2:
            ox, oc = diff_mixer(hx, hc, diff_w_in[j], diff_lambda[j], diff_subln_g[j], diff_w_out[j], i, ctx_out)
        else:
            ox, oc = na_mixer(hx, hc, na_w_in[j], na_rpb[j], na_w_out[j], ctx_out)
        x = x + g1 * ox
        x = x + g2 * conv_ffn(norm_modulate(x, norm2_g[i], sh2, sc2),
                              ffn_w_up[i], ffn_conv_w[i], ffn_conv_b[i], ffn_w_down[i])
        if ctx_out:
            ctx = ctx + cg1 * oc
            ctx = ctx + cg2 * conv_ffn(norm_modulate(ctx, norm2_g[i], csh2, csc2),
                                       ffn_w_up[i], ffn_conv_w[i], ffn_conv_b[i], ffn_w_down[i])
    return rms_norm(x, final_norm_g)


def setup_inputs(seed=0):
    out = dict(first_inputs(seed))
    for name, value in second_inputs(seed + 1).items():
        if name != "x":
            out[name + "_2"] = value
    return out


def reference(
    x, w_in, mix_scale, w_out, gdn_conv_w, gdn_a_log, gdn_dt_bias, gdn_norm_w, cnv_dw_w,
    cnv_dw_b, cnv_ln_g, cnv_ln_b, fox_f_bias, ln_mix_g, ln_mix_b, ln_ffn_g, ln_ffn_b, ffn_w1,
    ffn_w3, ffn_w2, moe_router, moe_w1, moe_w3, moe_w2, c_2, ctx_2, c_ctx_2, ada_w_2, ada_b_2,
    norm1_g_2, norm2_g_2, ffn_w_up_2, ffn_conv_w_2, ffn_conv_b_2, ffn_w_down_2, gqa_w_in_2,
    gqa_q_norm_g_2, gqa_k_norm_g_2, gqa_w_out_2, mla_w_in_2, mla_q_norm_g_2, mla_kv_norm_g_2,
    mla_w_uq_2, mla_w_ukv_2, mla_w_out_2, diff_w_in_2, diff_lambda_2, diff_subln_g_2,
    diff_w_out_2, na_w_in_2, na_rpb_2, na_w_out_2, final_norm_g_2,
):
    x = first_block(
        x, w_in, mix_scale, w_out, gdn_conv_w, gdn_a_log, gdn_dt_bias, gdn_norm_w, cnv_dw_w,
        cnv_dw_b, cnv_ln_g, cnv_ln_b, fox_f_bias, ln_mix_g, ln_mix_b, ln_ffn_g, ln_ffn_b,
        ffn_w1, ffn_w3, ffn_w2, moe_router, moe_w1, moe_w3, moe_w2,
    )
    return second_block(
        x, c_2, ctx_2, c_ctx_2, ada_w_2, ada_b_2, norm1_g_2, norm2_g_2, ffn_w_up_2,
        ffn_conv_w_2, ffn_conv_b_2, ffn_w_down_2, gqa_w_in_2, gqa_q_norm_g_2, gqa_k_norm_g_2,
        gqa_w_out_2, mla_w_in_2, mla_q_norm_g_2, mla_kv_norm_g_2, mla_w_uq_2, mla_w_ukv_2,
        mla_w_out_2, diff_w_in_2, diff_lambda_2, diff_subln_g_2, diff_w_out_2, na_w_in_2,
        na_rpb_2, na_w_out_2, final_norm_g_2,
    )


_drawn_inputs = setup_inputs


def setup_inputs(seed=0):
    import zlib

    import numpy as np

    out = dict(_drawn_inputs(seed))
    spreads = {}
    factors = {'mix_scale': 3.266,
     'gdn_norm_w': 4.116,
     'cnv_dw_b': 5.077,
     'cnv_ln_g': 4.997,
     'cnv_ln_b': 8.0,
     'norm1_g_2': 8.0,
     'norm2_g_2': 6.481,
     'ffn_conv_b_2': 7.099,
     'gqa_q_norm_g_2': 8.0,
     'gqa_k_norm_g_2': 8.0,
     'mla_q_norm_g_2': 8.0,
     'mla_kv_norm_g_2': 8.0,
     'final_norm_g_2': 2.787}
    for name, (base, spread) in spreads.items():
        noise = np.random.default_rng([zlib.crc32(name.encode()), seed]).standard_normal(out[name].shape)
        drawn = base * np.exp(spread * noise) if base else spread * noise
        out[name] = jnp.asarray(drawn.astype(out[name].dtype))
    for name, factor in factors.items():
        out[name] = (out[name] * factor).astype(out[name].dtype)
    return out
```

```python
from contextlib import ExitStack

import numpy as np

import concourse.bass as bass
from concourse import mybir

P = 128
F32 = mybir.dt.float32
ALU = mybir.AluOpType
ACT = mybir.ActivationFunctionType
AX = mybir.AxisListType.X

D = 1024
T = 256
TT = T // P
KD = D // P
H1 = 6
HD = 64
G = 12
CONVK = 31
F1 = 2816
KF = F1 // P
NE = 8
FE = 3584
KE = FE // P
ALPHA = 4 ** 0.25
RMS_EPS = 1e-6
LN_EPS = 1e-5
QH = 16

SLOT = 16
RING = 6
NBANK = 4

STAGES_A = [("in0", 25, 8), ("out0", 8, 8), ("up0", 2 * KF, 8), ("down0", 8, KF), ("in1", 25, 8), ("out1", 8, 8)]
MOE_TILES = 2 * KE + KD
MOE_SLOTS = (2 * KE * KD + KD * KE) // SLOT
STAGES_B = [("ada0", 48, 8), ("gin", 14, 8), ("gout", 8, 8), ("fup0", 2 * KF, 8), ("fdown0", 8, KF),
            ("ada1", 48, 8), ("min", 6, 8), ("uq", 16, 3), ("ukv", 16, 2), ("mout", 8, 8),
            ("fup1", 2 * KF, 8), ("fdown1", 8, KF)]


def plan():
    tile, slot = {}, {}
    t = s = 0
    last = []
    for group in (STAGES_A, None, STAGES_B):
        if group is None:
            tile["moe"], slot["moe"] = t, s
            t += NE * MOE_TILES
            s += NE * MOE_SLOTS
            last += [None] * (NE * MOE_SLOTS)
            continue
        for name, n, k in group:
            tile[name], slot[name] = t, s
            slots = -(-n * k // SLOT)
            last += [t + min(n * k - 1, SLOT * j + SLOT - 1) // k for j in range(slots)]
            t += n
            s += slots
    return tile, slot, last


TILE, SLOT0, LAST_TILE = plan()
N_A = SLOT0["moe"]
N_B = len(LAST_TILE) - N_A - NE * MOE_SLOTS


def moe_last(j):
    if j < 2 * KE * KD // SLOT:
        return 2 * j + 1
    return 2 * KE + (SLOT * (j - KE) + SLOT - 1) // KE


def columns(parts):
    at, out = 0, {}
    for name, n in parts:
        out[name] = at
        at += n
    return out, at


PV_PARTS = []
for _l in range(2):
    PV_PARTS += [(f"conv{_l}", 36), (f"mix{_l}", 8), (f"dw{_l}", 62), (f"dwb{_l}", 2), (f"clg{_l}", 2), (f"clb{_l}", 2),
                 (f"gnorm{_l}", 1), (f"lmg{_l}", 8), (f"lmb{_l}", 8), (f"lfg{_l}", 8), (f"lfb{_l}", 8)]
for _l in range(2):
    PV_PARTS += [(f"adab{_l}", 48), (f"n1g{_l}", 8), (f"n2g{_l}", 8), (f"fcw{_l}", 3 * 44), (f"fcb{_l}", 44)]
PV_PARTS += [("gqg", 1), ("gkg", 1), ("mqg", 3), ("mkg", 2), ("fing", 8)]
PV, NPV = columns(PV_PARTS)

CST_PARTS = [("ident", P), ("ones", P), ("triT", P), ("triS", P), ("m0", P), ("half0", P), ("half1", P), ("blk", P),
             ("tri", P), ("neg", P)] + [(f"m{k}T", P) for k in range(6)] + [
             ("rot64", P), ("rot96", P), ("cos64", T), ("sin64", T), ("cos96", T), ("sin96", T)]
CST, NCST = columns(CST_PARTS)


def build(nc, ws_a, ws_moe, ws_b, xT, ctxT, cT, pvec, prow, wsmall, wrouter, cst_d, out):
    with ExitStack() as ctx:
        sems = {}

        def sem(name):
            if name not in sems:
                sems[name] = ctx.enter_context(nc.semaphore(name))
            return sems[name]

        def sb(name, shape):
            return ctx.enter_context(nc.sbuf_tensor(name, shape, F32))

        ring = sb("ring", [P, RING * SLOT * P])
        X = sb("X_sb", [P, 2, KD, T])
        Y = sb("Y", [P, 2, KD, T])
        MIX = sb("MIX", [P, 2, KD, T])
        arena = sb("arena", [P, 22272])
        cst = sb("cst_sb", [P, NCST])
        pv = sb("pv", [P, NPV])
        pr = sb("pr", [P, 2, 24])
        wsm = sb("wsm", [P, 2, KD, 18])
        wrt = sb("wrt", [P, KD, NE])
        cvec = sb("cvec", [P, KD, 2])
        csil = sb("csil", [P, KD, 2])
        mod = sb("mod", [P, 48, 2])
        small = sb("small", [P, 640])
        P0 = ctx.enter_context(nc.psum_tensor("P0", [P, NBANK, 512], F32))
        P1 = ctx.enter_context(nc.psum_tensor("P1", [P, NBANK, 512], F32))
        P1f = P1[:, :, :].rearrange("p b c -> p (b c)")

        def arena_at(at, n):
            return arena[:, at:at + n]

        def c_(name, n=P):
            return cst[:, CST[name]:CST[name] + n]

        def v_(name, j=0, n=1):
            return pv[:, PV[name] + j:PV[name] + j + n]

        Yf = Y[:, :, :, :].rearrange("p s k t -> p (s k t)")
        Xf = X[:, :, :, :].rearrange("p s k t -> p (s k t)")
        Mf = MIX[:, :, :, :].rearrange("p s k t -> p (s k t)")
        x1, y1, mix1 = X[:, 1], Y[:, 1], MIX[:, 1]

        cpre = Yf[:, 0:9 * (T + 3)].rearrange("p (m t) -> p m t", m=9)
        gateS = Yf[:, 2400:2400 + 768]
        foxq = Mf[:, 0:768].rearrange("p (m t) -> p m t", m=3)
        foxk = Mf[:, 768:1536].rearrange("p (m t) -> p m t", m=3)
        UW = T + CONVK - 1
        upad = Xf[:, 0:2 * UW].rearrange("p (m t) -> p m t", m=2)
        cacc = Xf[:, 600:600 + 2 * T].rearrange("p (m t) -> p m t", m=2)
        foxvf = Xf[:, 1200:1200 + 768].rearrange("p (m t) -> p m t", m=3)
        qkvs = arena_at(0, 2304).rearrange("p (m t) -> p m t", m=9)
        tok = arena_at(2304, 2304)
        glub = arena_at(0, 512).rearrange("p (m t) -> p m t", m=2)
        csq = arena_at(512, 512).rearrange("p (m t) -> p m t", m=2)

        def xt(j):
            return arena_at(4608 + 768 * j, 768).rearrange("p (g d) -> p g d", g=G)

        qn, kn, kb, qe, kbe, kg, vb = [xt(j) for j in range(7)]
        U, vn, O1 = qn, kn, kb
        FM = arena_at(9984, 3072).rearrange("p (k r t) -> p k r t", k=4, r=6)
        WT = FM[:, 1]

        def bd(j):
            return arena_at(13056 + 1536 * j, 1536)

        decT, LT, AT, XI, XT, MT = [bd(j) for j in range(6)]
        YB = arena_at(0, 1536)

        def g3(ap):
            return ap.rearrange("p (g c) -> p g c", g=G)

        P1g = P1[:, :, 0:384].rearrange("p b (h c) -> p h b c", h=3)

        def g4(ap):
            return ap.rearrange("p (h b c) -> p h b c", h=3, b=4)

        sm = small[:, 0:36].rearrange("p (t c) -> p t c", t=TT)
        smz = small[:, 36:72].rearrange("p (t c) -> p t c", t=TT)
        sma = small[:, 72:108].rearrange("p (t c) -> p t c", t=TT)
        sme = small[:, 108:144].rearrange("p (t c) -> p t c", t=TT)
        smn = small[:, 144:180].rearrange("p (t c) -> p t c", t=TT)
        nA = small[:, 180:186]
        gst = small[:, 192:204]
        bet = small[:, 204:216]
        gcs = small[:, 216:264]
        eg = small[:, 264:276]
        el = small[:, 276:288]
        ss = small[:, 288:312]
        EG = small[:, 312:324].rearrange("p (c h t) -> p c h t", c=2, h=3)
        SBD = small[:, 324:324]
        lft = small[:, 324:336].rearrange("p (t c) -> p t c", t=TT)
        cc = small[:, 336:348].rearrange("p (t c) -> p t c", t=TT)
        rt = small[:, 352:512]
        stat = small[:, 512:544]
        state = sb("state", [P, 3, P])
        rstd = sb("rstd", [P, 512])

        CR = decT.rearrange("p (h t) -> p h t", h=H1)
        foxA = arena_at(14592, 1536)
        foxV = arena_at(16128, 768).rearrange("p (t c) -> p t c", t=TT)
        SC = arena_at(17000, 1024).rearrange("p (b c) -> p b c", b=2)

        PB = arena_at(18100, 1536).rearrange("p (b c) -> p b c", b=3)
        PTB = arena_at(19700, 1024).rearrange("p (b c) -> p b c", b=2)
        HN = arena_at(0, 4096).rearrange("p (s k t) -> p s k t", s=2, k=KD)
        Q2 = arena_at(4096, 4096).rearrange("p (s k t) -> p s k t", s=2, k=KD)
        K2 = arena_at(8192, 2048).rearrange("p (s k t) -> p s k t", s=2, k=4)
        VF2 = arena_at(10240, 1024).rearrange("p (m t) -> p m t", m=2)
        V2 = arena_at(11264, 1024).rearrange("p (t c) -> p t c", t=4)
        RAW = arena_at(12288, 1024).rearrange("p (b t) -> p b t", b=2)
        SQ = arena_at(13312, 1024).rearrange("p (b t) -> p b t", b=2)
        ROT = arena_at(14336, 512).rearrange("p (b t) -> p b t", b=2)
        CQ = Yf[:, 0:768].rearrange("p (m t) -> p m t", m=3)
        CKV = Yf[:, 1024:2048].rearrange("p (m t) -> p m t", m=2)
        KR = Yf[:, 2048:2560]
        MQ = arena_at(4096, 4096).rearrange("p (h t) -> p h t", h=QH)
        MK = arena_at(8192, 8192).rearrange("p (h t) -> p h t", h=QH)
        MV = arena_at(0, 4096).rearrange("p (t c) -> p t c", t=4)
        MTMP = arena_at(16384, 1536).rearrange("p (b t) -> p b t", b=3)
        HID = arena_at(4096, 11264)
        FS = arena_at(15360, 4096).rearrange("p (b t) -> p b t", b=8)
        SQN = arena_at(4096, 4096)
        MHID = arena_at(0, KE * T).rearrange("p (m t) -> p m t", m=KE)
        GR = arena_at(8192, 2048).rearrange("p (e t) -> p e t", e=NE)
        GD = arena_at(10240, 2048).rearrange("p (e t c) -> p e t c", e=NE, t=TT)

        class Count:

            def __init__(self, eng, own):
                self.eng, self.own, self.taken, self.made = eng, sem(own), {}, {}

            def take(self, name, n=1):
                self.taken[name] = self.taken.get(name, 0) + n
                self.eng.wait_ge(sem(name), self.taken[name])

            def link(self, ins, name=None):
                s = sem(name) if name else self.own
                self.made[s.name] = self.made.get(s.name, 0) + 1
                ins.then_inc(s, 1)
                self.eng.wait_ge(s, self.made[s.name])

        def tile_ready(eng, i):
            eng.wait_ge(sem("tile_done"), i + 1)

        def evac(i, b):
            return sem(f"evacuated{b}")

        def tile_out(ins, i):
            ins.then_inc(sem(f"evacuated{i % NBANK}"), 1)

        def wait_out(eng, i):
            eng.wait_ge(sem(f"evacuated{i % NBANK}"), i // NBANK + 1)

        def bank(i, n=512):
            return P0[:, i % NBANK, 0:n]

        def bc(ap, shape):
            return ap.to_broadcast(shape)

        block = ctx.enter_context(nc.Block())

        @block.sync
        def _(sp):
            def slot_dma(pos, src):
                return sp.dma_start(ring[:, pos * SLOT * P:(pos + 1) * SLOT * P], src)

            def stream(n, src, i):
                if n >= RING:
                    sp.wait_ge(sem("tile_done"), LAST_TILE[n - RING] + 1)
                slot_dma(n % RING, src[i]).then_inc(sem(f"weights{n % RING}"), 16)

            sp.dma_start(X[:, 1], xT).then_inc(sem("x_in"), 16)
            sp.dma_start(cst[:, :], cst_d).then_inc(sem("consts_in"), 16)
            sp.dma_start(pv[:, :], pvec).then_inc(sem("params_in"), 16)
            sp.dma_start(pr[:, :, :], prow).then_inc(sem("rows_in"), 16)
            sp.dma_start(wsm[:, :, :, :], wsmall).then_inc(sem("small_in"), 16)
            sp.dma_start(wrt[:, :, :], wrouter).then_inc(sem("router_in"), 16)
            sp.dma_start(cvec[:, :, :], cT).then_inc(sem("c_in"), 16)
            for n in range(N_A):
                stream(n, ws_a, n)
            with sp.Fori(0, NE) as e:
                for j in range(MOE_SLOTS):
                    n = N_A + j
                    if j >= RING:
                        sp.wait_ge(sem("tile_done"), e * MOE_TILES + (TILE["moe"] + moe_last(j - RING) + 1))
                    else:
                        sp.wait_ge(sem("tile_done"),
                                   e * MOE_TILES + (TILE["moe"] - MOE_TILES + moe_last(j - RING + MOE_SLOTS) + 1))
                    slot_dma(n % RING, ws_moe[bass.ds(e * MOE_SLOTS + j, 1)].rearrange("a p c -> (a p) c"))\
                        .then_inc(sem(f"weights{n % RING}"), 16)
            sp.wait_ge(sem("v_flipped"), 2)
            sp.wait_ge(sem("conv_normed"), 2)
            sp.dma_start(X[:, 0], ctxT).then_inc(sem("ctx_in"), 16)
            base = N_A + NE * MOE_SLOTS
            for i in range(N_B):
                n = base + i
                if i < RING:
                    sp.wait_ge(sem("tile_done"), TILE["moe"] + (NE - 1) * MOE_TILES + moe_last(MOE_SLOTS - RING + i) + 1)
                    slot_dma(n % RING, ws_b[i]).then_inc(sem(f"weights{n % RING}"), 16)
                else:
                    stream(n, ws_b, i)
            for t in range(TT):
                sp.wait_ge(sem("out_ready"), t + 1)
                sp.dma_start(out[t * P:(t + 1) * P, :], Yf[:, t * D:(t + 1) * D]).then_inc(sem("stored"), 16)
            sp.wait_ge(sem("stored"), 16 * TT)

        @block.tensor
        def _(pe):
            C = Count(pe, "pe_own")

            def weights(n):
                pe.wait_ge(sem(f"weights{n % RING}"), 16 * (n // RING + 1))

            def blockap(n, j):
                at = (n % RING) * SLOT * P + j * P
                return ring[:, at:at + P]

            def linear(name, tiles, k, rhs, n, first=0):
                for m in range(first, first + tiles):
                    i = TILE[name] + m
                    if i >= NBANK:
                        pe.wait_ge(sem(f"evacuated{i % NBANK}"), i // NBANK)
                    for kk in range(k):
                        b = m * k + kk
                        s = SLOT0[name] + b // SLOT
                        if b % SLOT == 0:
                            weights(s)
                        ins = nc.tensor.matmul(bank(i, n), blockap(s, b % SLOT), rhs(kk),
                                               start=kk == 0, stop=kk == k - 1)
                    ins.then_inc(sem("tile_done"), 1)

            def sums(name_in, k, rhs, n, out_ap, name_out, lhs=None):
                if name_in:
                    C.take(name_in)
                for kk in range(k):
                    ins = nc.tensor.matmul(out_ap, c_("ones") if lhs is None else lhs, rhs(kk),
                                           start=kk == 0, stop=kk == k - 1)
                ins.then_inc(sem(name_out), 1)

            def layer_norm(name_in, k, src, n):
                sums(name_in, k, src[0], n, P1[:, 0, 0:n], "ln_mean")
                sums("ln_sq", k, src[1], n, P1[:, 1, 0:n], "ln_var")

            def attention(units, qk, vfn, ks, rows):
                def scores(u):
                    if u >= 3:
                        C.take("scores_read")
                    q, kk, n = qk(u)
                    nc.tensor.matmul(P1[:, u % 3, 0:n], q, kk, start=True, stop=True).then_inc(sem("scores"), 1)

                def flip(u):
                    C.take("probs")
                    nk = units[u][2]
                    for j in range(nk):
                        ins = nc.tensor.transpose(P0[:, 2 + u % 2, j * P:(j + 1) * P], PB[:, u % 3, j * P:(j + 1) * P],
                                                  c_("ident"))
                    ins.then_inc(sem("probs_flipped"), 1)

                def values(u):
                    C.take("probsT")
                    if u >= 2:
                        C.take("heads_read")
                    nk = units[u][2]
                    r = rows(u)
                    for j in range(nk):
                        ins = nc.tensor.matmul(P0[r:r + HD, u % 2, 0:P], vfn(u, j), PTB[:, u % 2, j * P:(j + 1) * P],
                                               start=j == 0, stop=j == nk - 1)
                    ins.then_inc(sem("heads_out"), 1)

                n = len(units)
                for u in range(n + 2):
                    if u < n:
                        scores(u)
                    if 1 <= u < n + 1:
                        flip(u - 1)
                    if 2 <= u:
                        values(u - 2)
                C.take("scores_read", min(3, n))
                C.take("heads_read", 2)

            for name in ("x_in", "consts_in", "small_in"):
                pe.wait_ge(sem(name), 16)

            for l in range(2):
                if l:
                    C.take("x_ready")
                for t in range(TT):
                    for k in range(KD):
                        ins = nc.tensor.matmul(P1[:, 0, 32 * t:32 * t + 18], x1[:, k, t * P:(t + 1) * P], wsm[:, l, k, :],
                                               start=k == 0, stop=k == KD - 1)
                ins.then_inc(sem("gates_raw"), 1)
                linear(f"in{l}", 25, KD, lambda k: x1[:, k, :], T)
                C.take("qkv_act")
                for grp in range(5):
                    for j in range(min(4, 18 - 4 * grp)):
                        i = 4 * grp + j
                        if grp == 4 and j == 0:
                            C.take("tok_read")
                        ins = nc.tensor.transpose(P1[:, grp % 4, j * P:(j + 1) * P],
                                                  qkvs[:, i // 2, (i % 2) * P:(i % 2 + 1) * P], c_("ident"))
                    if grp >= 3:
                        ins.then_inc(sem("tok_flipped"), 1)
                C.take("decay_in")
                C.take("tok_read")
                for j, mname in enumerate(("triT", "blk", "half0", "half1")):
                    ins = nc.tensor.matmul(P1[:, 3, j * G:(j + 1) * G], c_(mname), gst, start=True, stop=True)
                for j in range(3):
                    ins = nc.tensor.matmul(P1[:, j, :], c_("ones"), YB[:, j * 512:(j + 1) * 512], start=True, stop=True)
                ins.then_inc(sem("decay_sums"), 1)
                for rnd in range(2):
                    C.take("fm_in")
                    if rnd:
                        C.take("fm_ready")
                    for j in range(2):
                        src = ((kn, kb), (qn, qe))[rnd][j]
                        for r in range(6):
                            at = (j * 6 + r) * P
                            ins = nc.tensor.transpose(P1f[:, at:at + P],
                                                      src[:, 2 * r:2 * r + 2, :].rearrange("p g d -> p (g d)"), c_("ident"))
                    ins.then_inc(sem("fm_flipped"), 1)
                C.take("fm_ready")
                for step, (a, b) in enumerate(((0, 1), (1, 0), (0, 2))):
                    if step:
                        C.take("gram_read")
                    for g in range(G):
                        hp, t, par = g // 4, (g // 2) % 2, g % 2
                        r = par * HD
                        ins = nc.tensor.matmul(P1[:, t * 2 + par, hp * P:(hp + 1) * P], FM[r:r + HD, a, hp * 2 + t, :],
                                               FM[r:r + HD, b, hp * 2 + t, :], start=True, stop=True)
                    ins.then_inc(sem("gram"), 1)
                C.take("gram_read")
                for lev in range(1, 6):
                    C.take("level_in")
                    for g in range(G):
                        ins = nc.tensor.matmul(P1f[:, g * P:(g + 1) * P], g3(MT)[:, g], g3(XI)[:, g], start=True, stop=True)
                    ins.then_inc(sem("inv_y"), 1)
                    C.take("inv_y_read")
                    if lev < 5:
                        for g in range(G):
                            ins = nc.tensor.matmul(P1f[:, g * P:(g + 1) * P], g3(XT)[:, g], g3(YB)[:, g],
                                                   start=True, stop=True)
                        ins.then_inc(sem("inv_z"), 1)
                        C.take("inv_z_read")
                    for g in range(G):
                        ins = nc.tensor.matmul(P1f[:, g * P:(g + 1) * P], g3(YB)[:, g], g3(XT)[:, g], start=True, stop=True)
                    ins.then_inc(sem("inv_zt"), 1)
                C.take("inverse")
                for g in range(G):
                    nc.tensor.matmul(P1f[:, g * HD:(g + 1) * HD], g3(XT)[:, g], vb[:, g], start=True, stop=True)
                for g in range(G):
                    hp, t, par = g // 4, (g // 2) % 2, g % 2
                    at = 1024 + (hp * 2 + t) * P
                    ins = nc.tensor.matmul(P1f[par * HD:(par + 1) * HD, at:at + P], kbe[:, g], g3(XT)[:, g],
                                           start=True, stop=True)
                ins.then_inc(sem("uw"), 1)
                C.take("u_ready")
                C.take("w_ready")
                for n in range(4):
                    t, c = n // 2, (n % 2) * HD
                    for hp in range(3):
                        ins = nc.tensor.matmul(P1[c:c + HD, 0, hp * P:(hp + 1) * P], WT[:, hp * 2 + t, c:c + HD],
                                               state[:, hp, :], start=True, stop=True)
                    ins.then_inc(sem("ws"), 1)
                    if n:
                        C.take("qs_read")
                    for hp in range(3):
                        ins = nc.tensor.matmul(P1[c:c + HD, 1, hp * P:(hp + 1) * P], FM[:, 3, hp * 2 + t, c:c + HD],
                                               state[:, hp, :], start=True, stop=True)
                    ins.then_inc(sem("qs"), 1)
                    C.take("v_new")
                    if n < 3:
                        for g in range(G):
                            hp, tg, par = g // 4, (g // 2) % 2, g % 2
                            if tg == t:
                                ins = nc.tensor.matmul(P1[par * HD:(par + 1) * HD, 2, hp * HD:(hp + 1) * HD],
                                                       kg[c:c + HD, g], vn[c:c + HD, g], start=True, stop=True)
                        ins.then_inc(sem("state_add"), 1)
                        C.take("state_ready")
                C.take("qs_read")
                for g in range(G):
                    ins = nc.tensor.matmul(P1f[:, g * HD:(g + 1) * HD], g3(AT)[:, g], vn[:, g], start=True, stop=True)
                ins.then_inc(sem("intra"), 1)
                C.take("delta_out")
                for r in range(6):
                    ins = nc.tensor.transpose(P1f[:, 1024 + r * P:1024 + (r + 1) * P],
                                              O1[:, 2 * r:2 * r + 2, :].rearrange("p g d -> p (g d)"), c_("ident"))
                ins.then_inc(sem("delta_flipped"), 1)
                C.take("delta_read")
                layer_norm("conv_out", 2, (lambda k: cacc[:, k, :], lambda k: csq[:, k, :]), T)
                C.take("forget_in")
                C.take("conv_normed")
                nc.tensor.matmul(P1[:, 3, 0:6], c_("tri"), lft[:, 0], start=True, stop=True)
                nc.tensor.matmul(P1[:, 3, 6:12], c_("tri"), lft[:, 1], start=True, stop=False)
                nc.tensor.matmul(P1[:, 3, 6:12], c_("ones"), lft[:, 0], start=False, stop=True)
                for j in range(3):
                    ins = nc.tensor.matmul(P1[:, j, :], c_("ones"), foxA[:, j * 512:(j + 1) * 512], start=True, stop=True)
                ins.then_inc(sem("forget_sums"), 1)
                C.take("forget_read")
                for m in range(3):
                    for t in range(TT):
                        i = m * TT + t
                        ins = nc.tensor.transpose(P1[:, i // 4, (i % 4) * P:(i % 4 + 1) * P],
                                                  foxvf[:, m, t * P:(t + 1) * P], c_("ident"))
                ins.then_inc(sem("v_flipped"), 1)
                C.take("v_ready")
                for b in range(NBANK):
                    i = TILE[f"in{l}"] + 24 - b
                    wait_out(pe, i)
                units = [(h, t, t + 1) for h in range(H1) for t in range(TT)]
                attention(units,
                          lambda u: (foxq[(units[u][0] % 2) * HD:(units[u][0] % 2 + 1) * HD, units[u][0] // 2,
                                          units[u][1] * P:(units[u][1] + 1) * P],
                                     foxk[(units[u][0] % 2) * HD:(units[u][0] % 2 + 1) * HD, units[u][0] // 2,
                                          0:units[u][2] * P], units[u][2] * P),
                          lambda u, j: foxV[:, j, units[u][0] * HD:(units[u][0] + 1) * HD],
                          None, lambda u: (units[u][0] % 2) * HD)
                linear(f"out{l}", 8, KD, lambda k: mix1[:, k, :], T)
                for m in range(KD - NBANK, KD):
                    wait_out(pe, TILE[f"out{l}"] + m)
                layer_norm(None, KD, (lambda k: y1[:, k, :], lambda k: SQN[:, k * T:(k + 1) * T]), T)
                C.take("x_ready")
                if l == 0:
                    linear("up0", 2 * KF, KD, lambda k: x1[:, k, :], T)
                    for m in (2 * KF - 3, 2 * KF - 1):
                        wait_out(pe, TILE["up0"] + m)
                    linear("down0", 8, KF, lambda k: HID[:, k * T:(k + 1) * T], T)
                    for m in range(KD - NBANK, KD):
                        wait_out(pe, TILE["down0"] + m)
                else:
                    pe.wait_ge(sem("router_in"), 16)
                    for t in range(TT):
                        for k in range(KD):
                            ins = nc.tensor.matmul(P1[:, 0, 8 * t:8 * t + 8], x1[:, k, t * P:(t + 1) * P], wrt[:, k, :],
                                                   start=k == 0, stop=k == KD - 1)
                    ins.then_inc(sem("logits"), 1)
                    C.take("gates_diag")
                    for j in range(4):
                        ins = nc.tensor.matmul(P1[:, j, :], c_("ones"),
                                               GD[:, 2 * j:2 * j + 2].rearrange("p e t c -> p (e t c)"),
                                               start=True, stop=True)
                    ins.then_inc(sem("gate_rows"), 1)
                    base = TILE["moe"]
                    with pe.Fori(0, NE) as e:
                        for m in range(MOE_TILES):
                            b = (base + m) % NBANK
                            pe.wait_ge(sem(f"evacuated{b}"), e * (MOE_TILES // NBANK) + (base + m) // NBANK)
                            up = m < 2 * KE
                            if m == 2 * KE:
                                for i in (base + m - 3, base + m - 1):
                                    pe.wait_ge(sem(f"evacuated{i % NBANK}"), e * (MOE_TILES // NBANK) + i // NBANK + 1)
                            k = KD if up else KE
                            first = m * KD if up else 2 * KE * KD + (m - 2 * KE) * KE
                            for kk in range(k):
                                j = (first + kk) // SLOT
                                n = N_A + j
                                if (first + kk) % SLOT == 0:
                                    pe.wait_ge(sem(f"weights{n % RING}"),
                                               e * (16 * MOE_SLOTS // RING) + 16 * (n // RING + 1))
                                rhs = x1[:, kk, :] if up else MHID[:, kk, :]
                                ins = nc.tensor.matmul(P0[:, b, 0:T], blockap(n, (first + kk) % SLOT), rhs,
                                                       start=kk == 0, stop=kk == k - 1)
                            ins.then_inc(sem("tile_done"), 1)
                    pe.wait_ge(sem("expert_added"), NE * KD)
                layer_norm(None, KD, (lambda k: y1[:, k, :], lambda k: SQN[:, k * T:(k + 1) * T]), T)

            C.take("x_ready")
            C.take("c_ready")
            pe.wait_ge(sem("ctx_in"), 16)
            for l in range(2):
                linear(f"ada{l}", 48, KD, lambda k: csil[:, k, :], 2)
                n = 2 * T

                def both(buf):
                    return lambda k: buf[:, :, k, :]

                sums("rms_in", KD, lambda k: SQN[:, k * 512:(k + 1) * 512], n, P1[:, 0, :], "rms_sum")
                C.take("normed")
                if l == 0:
                    def head_norm(m):
                        C.take("head_sq")
                        nc.tensor.matmul(P1[:, m % 2, :], c_("blk"), SQ[:, m % 2, :], start=True, stop=True)\
                            .then_inc(sem("head_sum"), 1)

                    def head_rot(m):
                        C.take("head_normed")
                        src = Q2[:, 1, m] if m < 8 else K2[:, 1, m - 8]
                        if m >= 2:
                            C.take("head_turned")
                        nc.tensor.matmul(P1[:, 2 + m % 2, 0:T], c_("rot64"), src, start=True, stop=True)\
                            .then_inc(sem("head_rotated"), 1)

                    for m in range(14):
                        linear("gin", 1, KD, both(HN), n, first=m)
                        if 1 <= m <= 12:
                            head_norm(m - 1)
                        if 2 <= m <= 13:
                            head_rot(m - 2)
                    C.take("head_turned", 2)
                    wait_out(pe, TILE["gin"] + 13)
                    wait_out(pe, TILE["gin"] + 12)
                    for m in range(2):
                        for t in range(4):
                            i = m * 4 + t
                            ins = nc.tensor.transpose(P1f[:, i * P:(i + 1) * P], VF2[:, m, t * P:(t + 1) * P], c_("ident"))
                    ins.then_inc(sem("v_flipped"), 1)
                    C.take("v_ready")
                    units = [(h, j, 2 if j < 2 else 4) for h in range(QH) for j in range(4)]

                    def qk(u):
                        h, j, nk = units[u]
                        r = (h % 2) * HD
                        q = Q2[r:r + HD, j // 2, h // 2, (j % 2) * P:(j % 2 + 1) * P]
                        return q, K2[r:r + HD, 0:nk // 2, h // 4, :], nk * P

                    attention(units, qk, lambda u, j: V2[:, j, (units[u][0] // 4) * HD:(units[u][0] // 4 + 1) * HD],
                              None, lambda u: (units[u][0] % 2) * HD)
                    linear("gout", 8, KD, both(MIX), n)
                    nf = n
                    sums("rms_in", KD, lambda k: SQN[:, k * 512:(k + 1) * 512], n, P1[:, 0, :], "rms_sum")
                    C.take("normed")
                    linear("fup0", 2 * KF, KD, both(HN), n)
                    C.take("gated", KF)
                    linear("fdown0", 8, KF, lambda k: HID[:, k * 512:(k + 1) * 512], n)
                else:
                    linear("min", 3, KD, lambda k: HN[:, 1, k, :], T)
                    linear("min", 3, KD, both(HN), n, first=3)
                    sums("lora_sq", 3, lambda k: MTMP[:, k, 0:T], T, P1[:, 0, 0:T], "lora_sum")
                    C.take("lora_normed")
                    sums("lora_sq", 2, lambda k: MTMP[:, k, :], n, P1[:, 1, :], "lora_sum")
                    C.take("lora_normed")
                    wait_out(pe, TILE["min"] + 5)
                    nc.tensor.matmul(P1[:, 2, 0:T], c_("rot96"), KR[:, T:2 * T], start=True, stop=True)\
                        .then_inc(sem("krope_rot"), 1)

                    def q_rot(h):
                        wait_out(pe, TILE["uq"] + h)
                        if h >= 2:
                            C.take("mq_turned")
                        nc.tensor.matmul(P1[:, h % 2, 0:T], c_("rot96"), MQ[:, h, :], start=True, stop=True)\
                            .then_inc(sem("mq_rot"), 1)

                    def v_flip(h):
                        wait_out(pe, TILE["ukv"] + h)
                        if h >= 2:
                            C.take("mv_read")
                        for t in range(4):
                            ins = nc.tensor.transpose(P1[:, h % 2, t * P:(t + 1) * P], MK[:, h, t * P:(t + 1) * P],
                                                      c_("ident"))
                        ins.then_inc(sem("mv_flipped"), 1)

                    for h in range(QH):
                        linear("uq", 1, 3, lambda k: CQ[:, k, :], T, first=h)
                        if h >= 1:
                            q_rot(h - 1)
                    q_rot(QH - 1)
                    C.take("mq_turned", 2)
                    C.take("krope_done")
                    for h in range(QH):
                        linear("ukv", 1, 2, lambda k: CKV[:, k, :], n, first=h)
                        if h >= 1:
                            v_flip(h - 1)
                    v_flip(QH - 1)
                    C.take("mv_read", 2)
                    C.take("mk_done")
                    units = [(h, j, 4) for h in range(QH) for j in range(2)]
                    attention(units, lambda u: (MQ[:, units[u][0], units[u][1] * P:(units[u][1] + 1) * P],
                                                MK[:, units[u][0], :], 4 * P),
                              lambda u, j: MV[:, j, units[u][0] * HD:(units[u][0] + 1) * HD],
                              None, lambda u: (units[u][0] % 2) * HD)
                    linear("mout", 8, KD, lambda k: mix1[:, k, :], T)
                    sums("rms_in", KD, lambda k: SQN[:, k * T:(k + 1) * T], T, P1[:, 0, 0:T], "rms_sum")
                    C.take("normed")
                    linear("fup1", 2 * KF, KD, lambda k: HN[:, 1, k, :], T)
                    C.take("gated", KF)
                    linear("fdown1", 8, KF, lambda k: HID[:, k * T:(k + 1) * T], T)
            sums("rms_in", KD, lambda k: SQN[:, k * T:(k + 1) * T], T, P1[:, 0, 0:T], "rms_sum")
            C.take("normed")
            for t in range(TT):
                for k in range(KD):
                    ins = nc.tensor.transpose(P1[:, 2 * t + k // 4, (k % 4) * P:(k % 4 + 1) * P],
                                              HN[:, 1, k, t * P:(t + 1) * P], c_("ident"))
                ins.then_inc(sem("out_flipped"), 1)

        @block.scalar
        def _(act):
            A = Count(act, "act_own")
            a = nc.scalar

            act.wait_ge(sem("params_in"), 16)
            act.wait_ge(sem("rows_in"), 16)
            act.wait_ge(sem("x_in"), 16)

            def attention(units, scale, src, heads):
                def flipped(u):
                    A.take("probs_flipped")
                    if u >= 2:
                        A.take("heads_out")
                    nk = units[u][2]
                    a.activation(PTB[:, u % 2, 0:nk * P], P0[:, 2 + u % 2, 0:nk * P], ACT.Copy).then_inc(sem("probsT"), 1)

                n = len(units)
                for u in range(n + 1):
                    if u < n:
                        A.take("row_max")
                        w = units[u][2] * P
                        a.activation(PB[:, u % 3, 0:w], src(u, w), ACT.Exp, bias=stat[:, u % 3:u % 3 + 1], scale=scale,
                                     accum_out=stat[:, 4 + u % 3:5 + u % 3]).then_inc(sem("exps"), 1)
                    if u >= 1:
                        flipped(u - 1)
                A.take("heads_out", min(2, n))

            def root(ap):
                A.take("inverse_var")
                A.link(a.activation(ap, ap, ACT.Sqrt), "inverse_std")

            def affine(dst, src, k, g, b):
                for kk in range(k):
                    ins = a.activation(dst[:, kk], src[:, kk], ACT.Identity, bias=v_(b, kk), scale=v_(g, kk))
                return ins

            for l in range(2):
                base = TILE[f"in{l}"]
                for m in range(9):
                    tile_ready(act, base + m)
                    tile_out(a.activation(cpre[:, m, 3:3 + T], bank(base + m, T), ACT.Copy), base + m)
                A.take("abs_ready")
                A.link(a.activation(sme, sma, ACT.Exp, scale=-1.0))
                A.link(a.activation(nA, pr[:, l, 18:24], ACT.Exp))
                a.activation(smn[:, :, 6:12], smz[:, :, 6:12], ACT.Exp, scale=-1.0).then_inc(sem("exp_gates"), 1)
                A.take("one_plus")
                a.activation(sma, sme, ACT.Ln).then_inc(sem("softplus"), 1)
                A.take("conv_qkv")
                A.link(a.activation(qkvs, qkvs, ACT.Silu), "qkv_act")
                for m in range(9, 13):
                    i = base + m
                    tile_ready(act, i)
                    if m < 11:
                        tile_out(a.activation(upad[:, m - 9, CONVK - 1:], bank(i, T), ACT.Copy), i)
                    else:
                        tile_out(a.activation(cacc[:, m - 11, :], bank(i, T), ACT.Sigmoid), i)
                for m in range(13, 16):
                    i = base + m
                    tile_ready(act, i)
                    tile_out(a.activation(gateS[:, (m - 13) * T:(m - 12) * T], bank(i, T), ACT.Silu), i)
                for m in range(16, 25):
                    i = base + m
                    tile_ready(act, i)
                    k, mm = (m - 16) // 3, (m - 16) % 3
                    dst = (foxq, foxk, foxvf)[k][:, mm, :]
                    tile_out(a.activation(dst, bank(i, T), ACT.Copy, scale=0.125 if k == 0 else 1.0), i)
                A.take("tok_flipped")
                A.link(a.activation(tok[:, 0:2048], P1f[:, :], ACT.Copy), "tok_read")
                A.take("tok_flipped")
                A.link(a.activation(tok[:, 2048:2304], P1f[:, 0:256], ACT.Copy), "tok_read")
                root(ss)
                A.take("diff")
                a.activation(decT, decT, ACT.Exp).then_inc(sem("decay_exp"), 1)
                A.take("diff_low")
                a.activation(MT, MT, ACT.Exp).then_inc(sem("decay_low_exp"), 1)
                A.take("decay_tok")
                A.link(a.activation(eg, gcs[:, 0:12], ACT.Exp))
                a.activation(el, el, ACT.Exp).then_inc(sem("decay_tok_exp"), 1)
                for par in range(2):
                    r = par * HD
                    for c in range(2):
                        A.link(a.activation(
                            EG[r:r + HD, c],
                            gcs[r:r + HD, 24 + 12 * c:36 + 12 * c].rearrange("p (h t q) -> p h t q", h=3, t=2)[:, :, :, par],
                            ACT.Exp), "chunk_exp")
                for rnd in range(2):
                    A.take("fm_flipped")
                    A.link(a.activation(FM[:, 2 * rnd:2 * rnd + 2].rearrange("p k r t -> p (k r t)"), P1f[:, 0:1536],
                                        ACT.Copy), "fm_ready")
                for lev in range(1, 6):
                    A.take("inv_y")
                    a.activation(YB, P1f[:, 0:1536], ACT.Copy).then_inc(sem("inv_y_read"), 1)
                A.take("uw")
                a.activation(U.rearrange("p g d -> p (g d)"), P1f[:, 0:768], ACT.Copy).then_inc(sem("u_ready"), 1)
                for n in range(4):
                    t, c = n // 2, (n % 2) * HD
                    A.take("qs")
                    dst = O1[c:c + HD].rearrange("p (h b) d -> p h (b d)", h=3)[:, :, t * P:(t + 1) * P]
                    A.link(a.activation(dst, P1[c:c + HD, 1, 0:384].rearrange("p (h d) -> p h d", h=3), ACT.Copy), "qs_read")
                root(ss[:, 0:12])
                A.take("ln_xc")
                A.link(a.activation(csq, cacc, ACT.Square), "ln_sq")
                root(rstd[:, 0:T])
                A.take("ln_scaled")
                for m in range(2):
                    A.link(a.activation(upad[:, m, 0:T], cacc[:, m], ACT.Silu, bias=v_(f"clb{l}", m), scale=v_(f"clg{l}", m)))
                for m in range(2):
                    ins = a.activation(mix1[:, 3 + m], upad[:, m, 0:T], ACT.Copy, scale=v_(f"mix{l}", 3 + m))
                A.link(ins, "conv_normed")
                A.take("v_flipped")
                A.link(a.activation(foxV.rearrange("p t (m c) -> p m t c", m=3),
                                    P1f[:, 0:768].rearrange("p (m t c) -> p m t c", m=3, t=2), ACT.Copy), "v_ready")
                units = [(h, t, t + 1) for h in range(H1) for t in range(TT)]
                attention(units, 1.0, lambda u, w: SC[:, u % 2, 0:w], H1)
                A.take("ln_xc")
                A.link(a.activation(SQN[:, 0:2048], y1.rearrange("p k t -> p (k t)"), ACT.Square), "ln_sq")
                root(rstd[:, 0:T])
                A.take("ln_scaled")
                A.link(affine(x1, y1, KD, f"lmg{l}", f"lmb{l}"), "x_ready")
                if l == 0:
                    for m in range(KF):
                        i = TILE["up0"] + 2 * m
                        tile_ready(act, i)
                        if m >= 4:
                            wait_out(act, i - 7)
                        tile_out(a.activation(FS[:, m % 4, 0:T], bank(i, T), ACT.Silu), i)
                else:
                    A.take("top_diff")
                    a.activation(rt[:, 64:66], rt[:, 64:66], ACT.Exp).then_inc(sem("top_exp"), 1)
                    A.take("gate_rows")
                    a.activation(GR.rearrange("p e t -> p (e t)"), P1f[:, :], ACT.Copy).then_inc(sem("gate_rows_read"), 1)
                    base = TILE["moe"]
                    with act.Fori(0, NE) as e:
                        for m in range(KE):
                            i = base + 2 * m
                            act.wait_ge(sem("tile_done"), e * MOE_TILES + i + 1)
                            j = i - 7 if m >= 4 else i - 7 + 2 * KE - MOE_TILES
                            act.wait_ge(sem(f"evacuated{j % NBANK}"), e * (MOE_TILES // NBANK) + j // NBANK + 1)
                            tile_out(a.activation(FS[:, m % 4, 0:T], bank(i, T), ACT.Silu), i)
                A.take("ln_xc")
                A.link(a.activation(SQN[:, 0:2048], y1.rearrange("p k t -> p (k t)"), ACT.Square), "ln_sq")
                root(rstd[:, 0:T])
                A.take("ln_scaled")
                A.link(affine(x1, y1, KD, f"lfg{l}", f"lfb{l}"), "x_ready")

            act.wait_ge(sem("c_in"), 16)
            A.link(a.activation(csil[:, :, :], cvec[:, :, :], ACT.Silu), "c_ready")
            act.wait_ge(sem("ctx_in"), 16)
            Sq3 = SQN.rearrange("p (k s t) -> p s k t", k=KD, s=2)

            def stage_out(name):
                for m in range(KD - NBANK, KD):
                    wait_out(act, TILE[name] + m)

            def square_stream(seg):
                if seg == 2:
                    for s in range(2):
                        A.link(a.activation(Sq3[:, s], X[:, s], ACT.Square), "rms_in" if s else None)
                    root(rstd[:, :])
                else:
                    A.link(a.activation(SQN[:, 0:2048], x1.rearrange("p k t -> p (k t)"), ACT.Square), "rms_in")
                    root(rstd[:, 0:T])

            for l in range(2):
                square_stream(2)
                if l == 0:
                    for m in range(14):
                        i = TILE["gin"] + m
                        tile_ready(act, i)
                        if m < 12:
                            if m >= 2:
                                A.take("head_normed")
                            tile_out(a.activation(RAW[:, m % 2, :], bank(i), ACT.Copy), i)
                            wait_out(act, i)
                            a.activation(SQ[:, m % 2, :], RAW[:, m % 2, :], ACT.Square).then_inc(sem("head_sq"), 1)
                        else:
                            A.take("head_normed")
                            tile_out(a.activation(VF2[:, m - 12, :], bank(i), ACT.Copy), i)
                        if 1 <= m <= 12:
                            root(rstd[:, :])
                    A.take("v_flipped")
                    A.link(a.activation(V2.rearrange("p t (m c) -> p m t c", m=2),
                                        P1f[:, 0:1024].rearrange("p (m t c) -> p m t c", m=2, t=4), ACT.Copy), "v_ready")
                    units = [(h, j, 2 if j < 2 else 4) for h in range(QH) for j in range(4)]
                    attention(units, 0.125, lambda u, w: P1[:, u % 3, 0:w], QH)
                    stage_out("gout")
                    square_stream(2)
                    for m in range(2 * KF):
                        i = TILE["fup0"] + m
                        tile_ready(act, i)
                        if m >= 4 and m % 2 == 0:
                            A.take("gated")
                        a.activation(FS[:, m % 4, :], bank(i), ACT.Identity, bias=v_("fcb0", m),
                                     scale=v_("fcw0", 3 * m + 1)).then_inc(sem("centre"), 1)
                        if m % 2:
                            wait_out(act, i)
                            a.activation(FS[:, 4 + (m // 2) % 2, :], FS[:, m % 4, :], ACT.Silu).then_inc(sem("gate_act"), 1)
                    A.take("gated", 2)
                else:
                    for m in range(6):
                        i = TILE["min"] + m
                        tile_ready(act, i)
                        dst = CQ[:, m, :] if m < 3 else (CKV[:, m - 3, :] if m < 5 else KR)
                        tile_out(a.activation(dst, bank(i, T if m < 3 else 512), ACT.Copy), i)
                    wait_out(act, TILE["min"] + 2)
                    wait_out(act, TILE["min"] + 1)
                    wait_out(act, TILE["min"])
                    A.link(a.activation(MTMP[:, :, 0:T], CQ, ACT.Square), "lora_sq")
                    root(rstd[:, 0:T])
                    A.take("lora_normed")
                    wait_out(act, TILE["min"] + 4)
                    wait_out(act, TILE["min"] + 3)
                    A.link(a.activation(MTMP[:, 0:2, :], CKV, ACT.Square), "lora_sq")
                    root(rstd[:, :])
                    for h in range(QH):
                        i = TILE["uq"] + h
                        tile_ready(act, i)
                        tile_out(a.activation(MQ[:, h, :], bank(i, T), ACT.Copy), i)
                    for h in range(QH):
                        i = TILE["ukv"] + h
                        tile_ready(act, i)
                        tile_out(a.activation(MK[:, h, :], bank(i), ACT.Copy), i)
                    units = [(h, j, 4) for h in range(QH) for j in range(2)]
                    attention(units, 96 ** -0.5, lambda u, w: P1[:, u % 3, 0:w], QH)
                    stage_out("mout")
                    square_stream(1)
                    for m in range(2 * KF):
                        i = TILE["fup1"] + m
                        tile_ready(act, i)
                        if m >= 4 and m % 2 == 0:
                            A.take("gated")
                        a.activation(FS[:, m % 4, 0:T], bank(i, T), ACT.Identity, bias=v_("fcb1", m),
                                     scale=v_("fcw1", 3 * m + 1)).then_inc(sem("centre"), 1)
                        if m % 2:
                            wait_out(act, i)
                            a.activation(FS[:, 4 + (m // 2) % 2, 0:T], FS[:, m % 4, 0:T], ACT.Silu)\
                                .then_inc(sem("gate_act"), 1)
                    A.take("gated", 2)
                stage_out(f"fdown{l}")
            square_stream(1)
            for t in range(TT):
                A.take("out_flipped")
                A.link(a.activation(Yf[:, t * D:(t + 1) * D], P1f[:, t * D:(t + 1) * D], ACT.Copy), "out_ready")

        @block.vector
        def _(dve):
            V = Count(dve, "dve_own")
            v = nc.vector
            L = V.link
            dve.wait_ge(sem("consts_in"), 16)
            dve.wait_ge(sem("params_in"), 16)
            dve.wait_ge(sem("rows_in"), 16)
            dve.wait_ge(sem("x_in"), 16)

            def inv_sqrt(dst, src, scale, eps):
                L(v.tensor_scalar(dst, src, scale, eps, ALU.mult, ALU.add))
                L(v.reciprocal(dst, dst), "inverse_var")
                V.take("inverse_std")

            def layer_norm(buf, k, width):
                V.take("ln_mean")
                L(v.tensor_scalar(rstd[:, 0:T], P1[:, 0, 0:T], 1.0 / width, None, ALU.mult))
                L(v.tensor_tensor(buf, buf, bc(rstd[:, 0:T].unsqueeze(1), [P, k, T]), ALU.subtract), "ln_xc")
                V.take("ln_var")
                inv_sqrt(rstd[:, 0:T], P1[:, 1, 0:T], 1.0 / width, LN_EPS)
                L(v.tensor_tensor(buf, buf, bc(rstd[:, 0:T].unsqueeze(1), [P, k, T]), ALU.mult), "ln_scaled")

            def gb(ap, c):
                return bc(ap.unsqueeze(2), [P, ap.shape[1], c])

            def mb(ap):
                return bc(ap.unsqueeze(1), [P, G, P])

            def attention(units, scale, prep, rows, out_ap, out_scale):
                def soft(u):
                    w = units[u][2] * P
                    src = prep(u, w)
                    L(v.tensor_reduce(stat[:, u % 3:u % 3 + 1], src, AX, ALU.max, negate=True))
                    L(v.tensor_scalar(stat[:, u % 3:u % 3 + 1], stat[:, u % 3:u % 3 + 1], scale, None, ALU.mult), "row_max")

                def norm(u):
                    w = units[u][2] * P
                    V.take("exps")
                    L(v.reciprocal(stat[:, 12 + u % 3:13 + u % 3], stat[:, 4 + u % 3:5 + u % 3]), "scores_read")
                    L(v.tensor_scalar(PB[:, u % 3, 0:w], PB[:, u % 3, 0:w], stat[:, 12 + u % 3:13 + u % 3], None, ALU.mult),
                      "probs")

                def put(u):
                    V.take("heads_out")
                    r = rows(u)
                    L(v.tensor_scalar(out_ap(u), P0[r:r + HD, u % 2, 0:P], out_scale(u), None, ALU.mult), "heads_read")

                n = len(units)
                for u in range(n + 3):
                    if u < n:
                        V.take("scores")
                        soft(u)
                    if u >= 3:
                        put(u - 3)
                    if 1 <= u <= n:
                        norm(u - 1)

            dve.wait_ge(sem("consts_in"), 16)
            L(v.memset(state[:, :, :], 0.0))
            for l in range(2):
                base = TILE[f"in{l}"]
                L(v.memset(cpre[:, :, 0:3], 0.0))
                L(v.memset(upad[:, :, 0:CONVK - 1], 0.0))
                if l:
                    L(v.memset(state[:, :, :], 0.0))
                V.take("gates_raw")
                L(v.tensor_tensor(smz, P1[:, 0, 0:64].rearrange("p (t c) -> p t c", t=2)[:, :, 0:18],
                                  bc(pr[:, l, 0:18].unsqueeze(1), [P, TT, 18]), ALU.add))
                L(v.scalar_tensor_tensor(sma, smz, -1.0, smz, ALU.mult, ALU.max), "abs_ready")
                V.take("exp_gates")
                L(v.tensor_scalar(sme, sme, 1.0, None, ALU.add), "one_plus")
                V.take("softplus")
                L(v.tensor_scalar(sm[:, :, 0:6], smz[:, :, 0:6], 0.0, None, ALU.max))
                L(v.tensor_tensor(sm[:, :, 0:6], sm[:, :, 0:6], sma[:, :, 0:6], ALU.add))
                L(v.tensor_tensor(sm[:, :, 0:6], sm[:, :, 0:6], bc(nA.unsqueeze(1), [P, TT, 6]), ALU.mult))
                for t in range(TT):
                    L(v.tensor_scalar(gst.rearrange("p (h t q) -> p h t q", h=3, t=2)[:, :, t],
                                      sm[:, t, 0:6].rearrange("p (h q) -> p h q", q=2), -1.0, None, ALU.mult))
                L(v.tensor_scalar(smn[:, :, 6:12], smn[:, :, 6:12], 1.0, None, ALU.add))
                for t in range(TT):
                    L(v.reciprocal(bet.rearrange("p (h t q) -> p h t q", h=3, t=2)[:, :, t],
                                   smn[:, t, 6:12].rearrange("p (h q) -> p h q", q=2)))
                L(v.tensor_scalar(lft, smz[:, :, 12:18], 0.0, None, ALU.min))
                L(v.tensor_tensor(lft, lft, sma[:, :, 12:18], ALU.subtract))
                for m in range(9):
                    wait_out(dve, base + m)
                    w = PV[f"conv{l}"] + 4 * m
                    L(v.tensor_scalar(qkvs[:, m, :], cpre[:, m, 3:3 + T], pv[:, w + 3:w + 4], None, ALU.mult))
                    for j in range(3):
                        L(v.scalar_tensor_tensor(qkvs[:, m, :], cpre[:, m, 2 - j:2 - j + T], pv[:, w + 2 - j:w + 3 - j],
                                                 qkvs[:, m, :], ALU.mult, ALU.add),
                          "conv_qkv" if m == 8 and j == 2 else None)
                V.take("tok_read", 2)
                tokg = tok.rearrange("p (g d) -> p g d", d=HD)
                sqv = arena_at(0, 1536)
                L(v.tensor_tensor(sqv, tok[:, 0:1536], tok[:, 0:1536], ALU.mult))
                L(v.tensor_reduce(ss, sqv.rearrange("p (g d) -> p g d", d=HD), AX, ALU.add))
                L(v.tensor_tensor(g3(YB), mb(c_("triT")), gb(gst, P), ALU.mult), "decay_in")
                inv_sqrt(ss, ss, 1.0, RMS_EPS)
                L(v.tensor_scalar(ss[:, 0:12], ss[:, 0:12], HD ** -0.5, None, ALU.mult))
                L(v.tensor_tensor(kn, tokg[:, 12:24], gb(ss[:, 12:24], HD), ALU.mult))
                V.take("decay_sums")
                L(v.tensor_copy(gcs, P1[:, 3, 0:48]))
                L(v.tensor_tensor(el, gcs[:, 12:24], gcs[:, 0:12], ALU.subtract), "decay_tok")
                L(v.tensor_tensor(g3(decT), P1f[:, 0:1536].rearrange("p (g c) -> p g c", g=G), gb(gcs[:, 0:12], P),
                                  ALU.subtract))
                L(v.scalar_tensor_tensor(g3(MT), g3(decT), -1.0, mb(c_("m0")), ALU.mult, ALU.mult), "diff_low")
                L(v.tensor_tensor(g3(decT), g3(decT), mb(c_("triT")), ALU.mult), "diff")
                L(v.tensor_tensor(kb, kn, gb(bet, HD), ALU.mult), "fm_in")
                L(v.tensor_tensor(qn, tokg[:, 0:12], gb(ss[:, 0:12], HD), ALU.mult))
                V.take("decay_tok_exp")
                V.take("chunk_exp", 4)
                L(v.tensor_tensor(qe, qn, gb(eg, HD), ALU.mult), "fm_in")
                L(v.tensor_tensor(kbe, kb, gb(eg, HD), ALU.mult))
                L(v.tensor_tensor(kg, kn, gb(el, HD), ALU.mult))
                L(v.tensor_tensor(vb, tokg[:, 24:36], gb(bet, HD), ALU.mult))
                V.take("decay_exp")
                L(v.tensor_tensor(g3(decT), g3(decT), mb(c_("triT")), ALU.mult))
                V.take("decay_low_exp")
                L(v.tensor_tensor(g3(MT), g3(MT), mb(c_("m0")), ALU.mult))
                V.take("gram")
                L(v.tensor_tensor(g4(LT), P1g, g4(decT), ALU.mult), "gram_read")
                L(v.tensor_tensor(g3(LT), g3(LT), mb(c_("triS")), ALU.mult))
                V.take("gram")
                L(v.tensor_tensor(g4(XI), P1g, g4(MT), ALU.mult), "gram_read")
                L(v.tensor_tensor(g3(XI), mb(c_("ident")), g3(XI), ALU.subtract))
                V.take("gram")
                L(v.tensor_tensor(g4(AT), P1g, g4(decT), ALU.mult), "gram_read")
                L(v.tensor_tensor(g3(XT), g3(LT), mb(c_("m0T")), ALU.mult))
                L(v.tensor_tensor(g3(XT), mb(c_("ident")), g3(XT), ALU.subtract))
                for lev in range(1, 6):
                    L(v.tensor_tensor(g3(MT), g3(LT), mb(c_(f"m{lev}T")), ALU.mult), "level_in")
                    if lev < 5:
                        V.take("inv_z")
                        L(v.tensor_tensor(XI, XI, P1f[:, 0:1536], ALU.subtract), "inv_z_read")
                    V.take("inv_zt")
                    L(v.tensor_tensor(XT, XT, P1f[:, 0:1536], ALU.subtract), "inverse" if lev == 5 else None)
                V.take("uw")
                L(v.tensor_copy(WT.rearrange("p r t -> p (r t)"), P1f[:, 1024:1792]), "w_ready")
                V.take("u_ready")
                for n in range(4):
                    t, c = n // 2, (n % 2) * HD
                    V.take("ws")
                    pick = [z[c:c + HD].rearrange("p (h b) d -> p h (b d)", h=3)[:, :, t * P:(t + 1) * P] for z in (vn, U)]
                    L(v.tensor_tensor(pick[0], pick[1], P1[c:c + HD, 0, 0:384].rearrange("p (h d) -> p h d", h=3),
                                      ALU.subtract), "v_new")
                    V.take("qs")
                    if n < 3:
                        for par in range(2):
                            r = par * HD
                            sd = state[r:r + HD, :, r:r + HD]
                            L(v.tensor_tensor(sd, sd, bc(EG[r:r + HD, n % 2, :, t].unsqueeze(2), [HD, 3, HD]), ALU.mult))
                        V.take("state_add")
                        for par in range(2):
                            r = par * HD
                            sd = state[r:r + HD, :, r:r + HD]
                            L(v.tensor_tensor(sd, sd, P1[r:r + HD, 2, 0:192].rearrange("p (h d) -> p h d", h=3), ALU.add),
                              "state_ready" if par else None)
                V.take("intra")
                V.take("qs_read", 4)
                O1f = O1.rearrange("p g d -> p (g d)")
                L(v.tensor_tensor(O1f, O1f, P1f[:, 0:768], ALU.add))
                L(v.tensor_tensor(U, O1, O1, ALU.mult))
                L(v.tensor_reduce(ss[:, 0:12], U, AX, ALU.add))
                inv_sqrt(ss[:, 0:12], ss[:, 0:12], 1.0 / HD, RMS_EPS)
                L(v.tensor_tensor(O1, O1, gb(ss[:, 0:12], HD), ALU.mult), "delta_out")
                for m in range(13, 16):
                    wait_out(dve, base + m)
                for m in range(3):
                    L(v.tensor_scalar(gateS[:, m * T:(m + 1) * T], gateS[:, m * T:(m + 1) * T], v_(f"mix{l}", m), None,
                                      ALU.mult))
                V.take("delta_flipped")
                L(v.scalar_tensor_tensor(mix1[:, 0:3].rearrange("p m t -> p (m t)"), P1f[:, 1024:1792],
                                         v_(f"gnorm{l}"), gateS, ALU.mult, ALU.mult), "delta_read")
                for m in range(9, 13):
                    wait_out(dve, base + m)
                uc = upad[:, :, CONVK - 1:]
                L(v.tensor_tensor(uc, uc, cacc, ALU.mult))
                for m in range(2):
                    w = PV[f"dw{l}"] + CONVK * m
                    L(v.tensor_scalar(cacc[:, m, :], upad[:, m, 0:T], pv[:, w:w + 1], v_(f"dwb{l}", m), ALU.mult, ALU.add))
                for j in range(1, CONVK):
                    for m in range(2):
                        w = PV[f"dw{l}"] + CONVK * m
                        ins = v.scalar_tensor_tensor(cacc[:, m, :], upad[:, m, j:j + T], pv[:, w + j:w + j + 1],
                                                     cacc[:, m, :], ALU.mult, ALU.add)
                        L(ins, "conv_out" if j == CONVK - 1 and m == 1 else None)
                layer_norm(cacc, 2, 2 * P)
                fa = foxA.rearrange("p (h t c) -> p h t c", h=H1, t=TT)
                for h in range(H1):
                    L(v.tensor_scalar(fa[:, h, 0], c_("tri"), lft[:, 0, h:h + 1], None, ALU.mult))
                    L(v.tensor_scalar(fa[:, h, 1], c_("tri"), lft[:, 1, h:h + 1], lft[:, 0, h:h + 1], ALU.mult, ALU.add),
                      "forget_in" if h == H1 - 1 else None)
                V.take("forget_sums")
                L(v.tensor_copy(cc.rearrange("p t c -> p (t c)"), P1[:, 3, 0:12]))
                L(v.tensor_copy(CR.rearrange("p h t -> p (h t)"), P1f[:, 0:1536]), "forget_read")
                units = [(h, t, t + 1) for h in range(H1) for t in range(TT)]

                def prep(u, w):
                    h, t, _ = units[u]
                    dst = SC[:, u % 2, 0:w]
                    L(v.scalar_tensor_tensor(dst, P1[:, u % 3, 0:w], cc[:, t, h:h + 1], CR[:, h, 0:w], ALU.add, ALU.subtract))
                    L(v.tensor_tensor(SC[:, u % 2, w - P:w], SC[:, u % 2, w - P:w], c_("neg"), ALU.add))
                    return dst

                attention(units, 1.0, prep, lambda u: (units[u][0] % 2) * HD,
                          lambda u: mix1[(units[u][0] % 2) * HD:(units[u][0] % 2 + 1) * HD, 5 + units[u][0] // 2,
                                         units[u][1] * P:(units[u][1] + 1) * P],
                          lambda u: pv[(units[u][0] % 2) * HD:(units[u][0] % 2 + 1) * HD,
                                       PV[f"mix{l}"] + 5 + units[u][0] // 2:PV[f"mix{l}"] + 6 + units[u][0] // 2])
                V.take("conv_normed")
                for m in range(KD):
                    i = TILE[f"out{l}"] + m
                    tile_ready(dve, i)
                    tile_out(v.scalar_tensor_tensor(y1[:, m], x1[:, m], ALPHA, bank(i, T), ALU.mult, ALU.add), i)
                for m in range(KD - NBANK, KD):
                    wait_out(dve, TILE[f"out{l}"] + m)
                layer_norm(y1, KD, D)
                V.take("x_ready")
                if l == 0:
                    for m in range(KF):
                        i = TILE["up0"] + 2 * m
                        tile_ready(dve, i + 1)
                        wait_out(dve, i)
                        tile_out(v.tensor_tensor(HID[:, m * T:(m + 1) * T], FS[:, m % 4, 0:T], bank(i + 1, T), ALU.mult), i + 1)
                    for m in range(KD):
                        i = TILE["down0"] + m
                        tile_ready(dve, i)
                        tile_out(v.scalar_tensor_tensor(y1[:, m], x1[:, m], ALPHA, bank(i, T), ALU.mult, ALU.add), i)
                    for m in range(KD - NBANK, KD):
                        wait_out(dve, TILE["down0"] + m)
                else:
                    V.take("logits")
                    lg = rt[:, 0:16].rearrange("p (t e) -> p t e", t=TT)
                    oh = [rt[:, 16 + 16 * j:32 + 16 * j].rearrange("p (t e) -> p t e", t=TT) for j in range(2)]
                    mx = [rt[:, 48 + 2 * j:50 + 2 * j] for j in range(2)]
                    tmp = rt[:, 80:96].rearrange("p (t e) -> p t e", t=TT)
                    rank = rt[:, 96:112].rearrange("p (t e) -> p t e", t=TT)
                    gates = rt[:, 112:128].rearrange("p (t e) -> p t e", t=TT)
                    L(v.tensor_copy(lg, P1[:, 0, 0:16].rearrange("p (t e) -> p t e", t=TT)))
                    for e in range(NE):
                        L(v.memset(rank[:, :, e:e + 1], float(NE - e)))
                    for j in range(2):
                        L(v.tensor_reduce(mx[j], lg, AX, ALU.max))
                        L(v.tensor_tensor(tmp, lg, bc(mx[j].unsqueeze(2), [P, TT, NE]), ALU.is_equal))
                        L(v.tensor_tensor(tmp, tmp, rank, ALU.mult))
                        L(v.tensor_reduce(rt[:, 52:54], tmp, AX, ALU.max))
                        L(v.tensor_tensor(oh[j], tmp, bc(rt[:, 52:54].unsqueeze(2), [P, TT, NE]), ALU.is_equal))
                        if j == 0:
                            L(v.tensor_scalar(tmp, oh[0], -3.0e38, None, ALU.mult))
                            L(v.tensor_tensor(lg, lg, tmp, ALU.add))
                    L(v.tensor_tensor(rt[:, 64:66], mx[1], mx[0], ALU.subtract), "top_diff")
                    V.take("top_exp")
                    L(v.tensor_scalar(rt[:, 66:68], rt[:, 64:66], 1.0, None, ALU.add))
                    L(v.reciprocal(rt[:, 68:70], rt[:, 66:68]))
                    L(v.tensor_tensor(rt[:, 70:72], rt[:, 68:70], rt[:, 64:66], ALU.mult))
                    L(v.tensor_tensor(gates, oh[0], bc(rt[:, 68:70].unsqueeze(2), [P, TT, NE]), ALU.mult))
                    L(v.tensor_tensor(tmp, oh[1], bc(rt[:, 70:72].unsqueeze(2), [P, TT, NE]), ALU.mult))
                    L(v.tensor_tensor(gates, gates, tmp, ALU.add))
                    for t in range(TT):
                        L(v.tensor_tensor(GD[:, :, t, :], bc(c_("ident").unsqueeze(1), [P, NE, P]),
                                          bc(gates[:, t].unsqueeze(2), [P, NE, P]), ALU.mult),
                          "gates_diag" if t else None)
                    L(v.tensor_scalar(y1, x1, ALPHA, None, ALU.mult))
                    V.take("gate_rows_read")
                    base = TILE["moe"]
                    with dve.Fori(0, NE) as e:
                        for m in range(KE):
                            i = base + 2 * m
                            b = i % NBANK
                            dve.wait_ge(sem("tile_done"), e * MOE_TILES + i + 2)
                            dve.wait_ge(sem(f"evacuated{b}"), e * (MOE_TILES // NBANK) + i // NBANK + 1)
                            tile_out(v.tensor_tensor(MHID[:, m], FS[:, m % 4, 0:T], bank(i + 1, T), ALU.mult), i + 1)
                        for m in range(KD):
                            i = base + 2 * KE + m
                            dve.wait_ge(sem("tile_done"), e * MOE_TILES + i + 1)
                            tile_out(v.tensor_tensor(FS[:, 4 + m % 2, 0:T], bank(i, T),
                                                     GR[:, bass.ds(e, 1), :].rearrange("p a t -> p (a t)"), ALU.mult), i)
                            dve.wait_ge(sem(f"evacuated{i % NBANK}"), e * (MOE_TILES // NBANK) + i // NBANK + 1)
                            v.tensor_tensor(y1[:, m], y1[:, m], FS[:, 4 + m % 2, 0:T], ALU.add)\
                                .then_inc(sem("expert_added"), 1)
                            dve.wait_ge(sem("expert_added"), e * KD + m + 1)
                layer_norm(y1, KD, D)
                V.take("x_ready")

            dve.wait_ge(sem("ctx_in"), 16)

            def both_rows(ap, k=KD):
                return ap

            def rms(segs, gname, shift, scale):
                V.take("rms_sum")
                n = len(segs) * T
                inv_sqrt(rstd[:, 0:n], P1[:, 0, 0:n], 1.0 / D, RMS_EPS)
                for j, s in enumerate(segs):
                    L(v.tensor_tensor(HN[:, s], X[:, s], bc(rstd[:, j * T:(j + 1) * T].unsqueeze(1), [P, KD, T]), ALU.mult))
                for s in segs:
                    col = 1 - s
                    for k in range(KD):
                        if scale is None:
                            ins = v.tensor_scalar(HN[:, s, k], HN[:, s, k], v_(gname, k), None, ALU.mult)
                        else:
                            ins = v.tensor_scalar(HN[:, s, k], HN[:, s, k], gs[:, k, col:col + 1],
                                                  mod[:, shift + k, col:col + 1], ALU.mult, ALU.add)
                        L(ins, "normed" if s == segs[-1] and k == KD - 1 else None)

            gs = rt[:, 0:16].rearrange("p (k c) -> p k c", c=2)

            def gain(gname, scale):
                L(v.tensor_scalar(gs, mod[:, scale:scale + KD, :], 1.0, None, ALU.add))
                L(v.tensor_tensor(gs, gs, bc(v_(gname, 0, KD).unsqueeze(2), [P, KD, 2]), ALU.mult))

            def residual(name, segs, gate):
                n = len(segs) * T
                for m in range(KD):
                    i = TILE[name] + m
                    tile_ready(dve, i)
                    for j, s in enumerate(segs):
                        ins = v.scalar_tensor_tensor(X[:, s, m], bank(i)[:, j * T:(j + 1) * T],
                                                     mod[:, gate + m, 1 - s:2 - s], X[:, s, m], ALU.mult, ALU.add)
                        if j == len(segs) - 1:
                            tile_out(ins, i)
                            wait_out(dve, i)
                        else:
                            L(ins)

            for l in range(2):
                for m in range(48):
                    i = TILE[f"ada{l}"] + m
                    tile_ready(dve, i)
                    tile_out(v.tensor_scalar(mod[:, m, :], bank(i, 2), v_(f"adab{l}", m), None, ALU.add), i)
                for m in range(44, 48):
                    wait_out(dve, TILE[f"ada{l}"] + m)
                gain(f"n1g{l}", 8)
                rms((0, 1), None, 0, 8)
                if l == 0:
                    def head_scale(m):
                        V.take("head_sum")
                        inv_sqrt(rstd[:, :], P1[:, m % 2, :], 1.0 / HD, RMS_EPS)
                        g = v_("gqg") if m < 8 else v_("gkg")
                        dst = Q2[:, :, m, :] if m < 8 else K2[:, :, m - 8, :]
                        L(v.scalar_tensor_tensor(dst, RAW[:, m % 2, :].rearrange("p (s t) -> p s t", s=2), g,
                                                 rstd[:, :].rearrange("p (s t) -> p s t", s=2), ALU.mult, ALU.mult),
                          "head_normed")

                    def head_turn(m):
                        V.take("head_rotated")
                        x = Q2[:, 1, m] if m < 8 else K2[:, 1, m - 8]
                        L(v.tensor_tensor(ROT[:, 0], P1[:, 2 + m % 2, 0:T], c_("sin64", T), ALU.mult))
                        L(v.tensor_tensor(ROT[:, 1], x, c_("cos64", T), ALU.mult))
                        L(v.tensor_tensor(x, ROT[:, 0], ROT[:, 1], ALU.add), "head_turned")

                    for m in range(13):
                        if m < 12:
                            head_scale(m)
                        if m >= 1:
                            head_turn(m - 1)
                    units = [(h, j, 2 if j < 2 else 4) for h in range(QH) for j in range(4)]
                    attention(units, 0.125, lambda u, w: P1[:, u % 3, 0:w], lambda u: (units[u][0] % 2) * HD,
                              lambda u: MIX[(units[u][0] % 2) * HD:(units[u][0] % 2 + 1) * HD, units[u][1] // 2,
                                            units[u][0] // 2, (units[u][1] % 2) * P:(units[u][1] % 2 + 1) * P],
                              lambda u: 1.0)
                    residual("gout", (0, 1), 16)
                    gain("n2g0", 32)
                    rms((0, 1), None, 24, 32)
                    segs = 2
                else:
                    def lora(buf, k, width, n, bnk, g):
                        V.take("lora_sum")
                        inv_sqrt(rstd[:, 0:n], P1[:, bnk, 0:n], 1.0 / width, RMS_EPS)
                        for kk in range(k):
                            L(v.scalar_tensor_tensor(buf[:, kk, :], buf[:, kk, :], v_(g, kk), rstd[:, 0:n],
                                                     ALU.mult, ALU.mult), "lora_normed" if kk == k - 1 else None)

                    lora(CQ, 3, 3 * P, T, 0, "mqg")
                    lora(CKV, 2, 2 * P, 2 * T, 1, "mkg")
                    V.take("krope_rot")
                    L(v.tensor_tensor(MTMP[:, 2, 0:T], P1[:, 2, 0:T], c_("sin96", T), ALU.mult))
                    L(v.tensor_tensor(KR[:, T:], KR[:, T:], c_("cos96", T), ALU.mult))
                    L(v.tensor_tensor(KR[:, T:], KR[:, T:], MTMP[:, 2, 0:T], ALU.add), "krope_done")
                    for h in range(QH):
                        V.take("mq_rot")
                        L(v.tensor_tensor(MTMP[:, 0, 0:T], P1[:, h % 2, 0:T], c_("sin96", T), ALU.mult))
                        L(v.tensor_tensor(MTMP[:, 1, 0:T], MQ[:, h], c_("cos96", T), ALU.mult))
                        L(v.tensor_tensor(MQ[:, h], MTMP[:, 0, 0:T], MTMP[:, 1, 0:T], ALU.add),
                          "mq_turned")
                    for h in range(QH):
                        V.take("mv_flipped")
                        L(v.tensor_copy(MV[:, :, h * HD:(h + 1) * HD],
                                        P1[:, h % 2, :].rearrange("p (t c) -> p t c", t=4)[:, :, HD:P]), "mv_read")
                        L(v.tensor_copy(MK[HD:P, h, :], KR[HD:P, :]), "mk_done" if h == QH - 1 else None)
                    units = [(h, j, 4) for h in range(QH) for j in range(2)]
                    attention(units, 96 ** -0.5, lambda u, w: P1[:, u % 3, 0:w], lambda u: (units[u][0] % 2) * HD,
                              lambda u: mix1[(units[u][0] % 2) * HD:(units[u][0] % 2 + 1) * HD, units[u][0] // 2,
                                             units[u][1] * P:(units[u][1] + 1) * P],
                              lambda u: 1.0)
                    residual("mout", (1,), 16)
                    gain("n2g1", 32)
                    rms((1,), None, 24, 32)
                    segs = 1
                n = segs * T
                w0 = PV[f"fcw{l}"]
                for m in range(2 * KF):
                    i = TILE[f"fup{l}"] + m
                    tile_ready(dve, i)
                    V.take("centre")
                    f3 = FS[:, m % 4, 0:n].rearrange("p (s t) -> p s t", s=segs)
                    b3 = bank(i, n).rearrange("p (s t) -> p s t", s=segs)
                    L(v.scalar_tensor_tensor(f3[:, :, 1:], b3[:, :, 0:T - 1], pv[:, w0 + 3 * m:w0 + 3 * m + 1], f3[:, :, 1:],
                                             ALU.mult, ALU.add))
                    ins = v.scalar_tensor_tensor(f3[:, :, 0:T - 1], b3[:, :, 1:], pv[:, w0 + 3 * m + 2:w0 + 3 * m + 3],
                                                 f3[:, :, 0:T - 1], ALU.mult, ALU.add)
                    tile_out(ins, i)
                    wait_out(dve, i)
                    if m % 2:
                        V.take("gate_act")
                        ins = v.tensor_tensor(HID[:, (m // 2) * n:(m // 2 + 1) * n], FS[:, (m - 1) % 4, 0:n],
                                              FS[:, 4 + (m // 2) % 2, 0:n], ALU.mult)
                        L(ins, "gated")
                residual(f"fdown{l}", (0, 1) if l == 0 else (1,), 40)
            rms((1,), "fing", None, None)


def tiles(w, starts, k, width=P):
    cols = []
    for st in starts:
        c = np.arange(st, st + P) if isinstance(st, int) else st
        t = np.zeros((k * P, P), np.float32)
        ok = c >= 0
        t[:, ok] = w[:, c[ok]]
        cols.append(t.reshape(k, P, P).transpose(1, 0, 2))
    a = np.concatenate(cols, axis=1)
    pad = -a.shape[1] % SLOT
    if pad:
        a = np.concatenate([a, np.zeros((P, pad, P), np.float32)], axis=1)
    return a.reshape(P, -1, SLOT * P).transpose(1, 0, 2)


def vec(v):
    return np.asarray(v).reshape(-1, P).T


def constants():
    i = np.arange(P)
    a, b = i[:, None], i[None, :]
    same = a // HD == b // HD
    out = {
        "ident": a == b, "ones": np.ones((P, P)), "triT": same & (a <= b), "triS": same & (a < b),
        "m0": (a == b + 1) & (a % 2 == 1), "half0": np.broadcast_to(a < HD, (P, P)),
        "half1": np.broadcast_to(a >= HD, (P, P)), "blk": same, "tri": a <= b, "neg": np.where(b > a, -1e30, 0.0),
    }
    for k in range(6):
        n = 2 ** k
        out[f"m{k}T"] = (a // (2 * n) == b // (2 * n)) & ((a // n) % 2 == 0) & ((b // n) % 2 == 1)
    t = np.arange(T)
    row, col = (t // 64).astype(np.float32), (t % 64).astype(np.float32)
    for dim, name, heads, at in ((64, "64", 2, 0), (32, "96", 1, 64)):
        half, q = dim // 2, dim // 4
        inv = (np.float32(10000.0) ** (-np.arange(0, half, 2, dtype=np.float32) / np.float32(half))).astype(np.float32)
        ar, ac = row[:, None] * inv, col[:, None] * inv
        ang = np.concatenate([ar, ar, ac, ac], axis=-1).T
        rot, cos, sin = np.zeros((P, P)), np.ones((P, T)), np.zeros((P, T))
        for h in range(heads):
            o = at + h * dim
            cos[o:o + dim], sin[o:o + dim] = np.cos(ang), np.sin(ang)
            for p in range(dim):
                if (p // q) % 2 == 0:
                    rot[o + p + q, o + p] = -1
                else:
                    rot[o + p - q, o + p] = 1
        out["rot" + name], out["cos" + name], out["sin" + name] = rot, cos, sin
    return np.concatenate([np.asarray(out[n], np.float32) for n, _ in CST_PARTS], axis=1)


def pairs(n, off):
    return [s for m in range(n) for s in (m * P, off + m * P)]


def kernel(**inputs):
    import concourse.bacc as bacc
    from concourse.bass_utils import run_bass_kernel_spmd

    z = {k: np.asarray(v) for k, v in inputs.items()}
    win = z["w_in"]
    in_cols = ([m * P for m in range(9)] + [1548 + m * P for m in range(4)] + [1164 + m * P for m in range(3)]
               + [2060 + m * P for m in range(9)])
    full = [m * P for m in range(KD)]

    def up_pair(a, b, n):
        both = np.concatenate([a, b], axis=1)
        return tiles(both, pairs(n, a.shape[1]), KD)

    ws_a = np.concatenate([
        tiles(win[0], in_cols, KD), tiles(z["w_out"][0], full, KD), up_pair(z["ffn_w1"][0], z["ffn_w3"][0], KF),
        tiles(z["ffn_w2"][0], full, KF), tiles(win[1], in_cols, KD), tiles(z["w_out"][1], full, KD)])

    w1 = z["moe_w1"][0].reshape(NE, KD, P, KE, P)
    w3 = z["moe_w3"][0].reshape(NE, KD, P, KE, P)
    up = np.stack([w1, w3], axis=1).transpose(0, 4, 3, 1, 2, 5).reshape(NE, KE, P, SLOT * P)
    down = z["moe_w2"][0].reshape(NE, KE, P, KD, P).transpose(0, 2, 3, 1, 4).reshape(NE, P, -1, SLOT * P)
    ws_moe = np.concatenate([up, down.transpose(0, 2, 1, 3)], axis=1).reshape(-1, P, SLOT * P)

    gq = z["gqa_w_in_2"][0]
    kdup = [np.tile(np.arange(1024 + h * HD, 1024 + (h + 1) * HD), 2) for h in range(4)]
    mi = z["mla_w_in_2"][0]
    rope_cols = np.full(P, -1)
    rope_cols[HD:HD + 32] = np.arange(640, 672)
    uq = z["mla_w_uq_2"][0]
    uq_cols = [np.concatenate([np.arange(h * 96, h * 96 + 96), np.full(32, -1)]) for h in range(QH)]

    def ffn(l):
        return [tiles(z["ffn_w_up_2"][l], pairs(KF, F1), KD), tiles(z["ffn_w_down_2"][l], full, KF)]

    ada = [tiles(z["ada_w_2"][l], [m * P for m in range(48)], KD) for l in range(2)]
    ws_b = np.concatenate(
        [ada[0], tiles(gq, full + kdup + [1280, 1408], KD), tiles(z["gqa_w_out_2"][0], full, KD)] + ffn(0)
        + [ada[1], tiles(mi, [0, P, 2 * P, 384, 512, rope_cols], KD), tiles(uq, uq_cols, 3),
           tiles(z["mla_w_ukv_2"][0], [m * P for m in range(16)], 2), tiles(z["mla_w_out_2"][0], full, KD)] + ffn(1))
    assert ws_a.shape[0] == N_A and ws_b.shape[0] == N_B and ws_moe.shape[0] == NE * MOE_SLOTS

    def heads(w):
        return np.concatenate([w[:, 1152:1164], w[:, 3212:3218]], axis=1).reshape(KD, P, 18).transpose(1, 0, 2)

    wsmall = np.stack([heads(win[l]) for l in range(2)], axis=1)
    zero6 = np.zeros(6, np.float32)
    prow = np.stack([np.concatenate([z["gdn_dt_bias"][l], zero6, z["fox_f_bias"][l], z["gdn_a_log"][l]]) for l in range(2)])
    prow = np.broadcast_to(prow, (P, 2, 24))

    def taps(w, order=None):
        a = w.reshape(w.shape[0], -1, P)
        if order is not None:
            a = a[:, order]
        return a.transpose(2, 1, 0).reshape(P, -1)

    inter = [j for m in range(KF) for j in (m, KF + m)]
    cols = []
    for l in range(2):
        cols += [taps(z["gdn_conv_w"][l]), vec(z["mix_scale"][l]), taps(z["cnv_dw_w"][l]), vec(z["cnv_dw_b"][l]),
                 vec(z["cnv_ln_g"][l]), vec(z["cnv_ln_b"][l]), np.tile(z["gdn_norm_w"][l], 2)[:, None],
                 vec(z["ln_mix_g"][l]), vec(z["ln_mix_b"][l]), vec(z["ln_ffn_g"][l]), vec(z["ln_ffn_b"][l])]
    for l in range(2):
        cols += [vec(z["ada_b_2"][l]), vec(z["norm1_g_2"][l]), vec(z["norm2_g_2"][l]),
                 taps(z["ffn_conv_w_2"][l], inter), vec(z["ffn_conv_b_2"][l])[:, inter]]
    cols += [np.tile(z["gqa_q_norm_g_2"][0], 2)[:, None], np.tile(z["gqa_k_norm_g_2"][0], 2)[:, None],
             vec(z["mla_q_norm_g_2"][0]), vec(z["mla_kv_norm_g_2"][0]), vec(z["final_norm_g_2"])]
    pvec = np.concatenate(cols, axis=1)
    assert pvec.shape == (P, NPV)

    def feature_major(a):
        return a.reshape(-1, KD, P).transpose(2, 1, 0)

    arrays = {
        "ws_a": ws_a, "ws_moe": ws_moe, "ws_b": ws_b,
        "xT": feature_major(z["x"][0]), "ctxT": feature_major(z["ctx_2"][0]),
        "cT": feature_major(np.stack([z["c_2"][0], z["c_ctx_2"]])),
        "pvec": pvec, "prow": prow, "wsmall": wsmall,
        "wrouter": z["moe_router"][0].reshape(KD, P, NE).transpose(1, 0, 2), "cst": constants(),
    }
    arrays = {k: np.ascontiguousarray(a) for k, a in arrays.items()}
    nc = bacc.Bacc("TRN2", target_bir_lowering=False, num_devices=1)
    args = [nc.dram_tensor(k, a.shape, F32, kind="ExternalInput").ap() for k, a in arrays.items()]
    out = nc.dram_tensor("out", (T, D), F32, kind="ExternalOutput").ap()
    build(nc, *args, out)
    r = run_bass_kernel_spmd(nc, [arrays], core_ids=[0])
    return r.results[0]["out"].reshape(1, T, D)
```
